# Optimizing a Trainium2 kernel written in Bass

```python
import jax, jax.numpy as jnp
from jax import lax
import numpy as np

D_MODEL = 1024
BATCH = 1
SEQ = 256
DEPTH = 4
DEC_BATCH = 1
DEC_SEQ = 64
PAST_LEN = 128

CHUNK = 64
N_MIXERS = 3
N_A = (DEPTH + 2) // 3
N_B = (DEPTH + 1) // 3
N_C = DEPTH // 3
NORM_EPS = 1e-6
ROPE_THETA = 500000.0
Q_BLOCK = 128

A_HEADS = 16
A_HEAD_DIM = 64
A_KV_HEADS = 2
A_ROT = A_HEAD_DIM // 4
IDX_HEADS = 8
IDX_DIM = 64
IDX_ROT = IDX_DIM // 4
TOPK_MAX = 256
A_O_Q = A_HEADS * A_HEAD_DIM
A_O_K = A_O_Q + A_KV_HEADS * A_HEAD_DIM
A_O_V = A_O_K + A_KV_HEADS * A_HEAD_DIM
A_O_QI = A_O_V + IDX_HEADS * IDX_DIM
A_O_KI = A_O_QI + IDX_DIM
A_IN = A_O_KI + IDX_HEADS

B_HEAD_DIM = 64
B_HEADS = D_MODEL // B_HEAD_DIM
B_DECAY_LORA = 64
B_ICL_LORA = 64
B_GATE_LORA = 128
B_GN_EPS = 64e-5

C_HEADS = 16
C_NOPE = 64
C_ROPE = 32
C_V = 64
C_Q_RANK = 512
C_KV_RANK = 256
C_IN = C_Q_RANK + C_KV_RANK + C_ROPE

D_FF = 2816
CONV_W = 3

kernel_name = 'hybrid_dsa_rwkv7_mla_convffn_step'

F32 = jnp.float32

def _rmsnorm(x, g):
    xf = x.astype(F32)
    xf = xf * lax.rsqrt(jnp.mean(xf * xf, axis=-1, keepdims=True) + NORM_EPS)
    return xf.astype(x.dtype) * g

def _rope(x, pos, rot):
    half = rot // 2
    inv = ROPE_THETA ** (-jnp.arange(half, dtype=F32) / half)
    ang = pos.astype(F32)[:, None] * inv[None, :]
    shape = (ang.shape[0],) + (1,) * (x.ndim - 3) + (half,)
    cos = jnp.cos(ang).reshape(shape).astype(x.dtype)
    sin = jnp.sin(ang).reshape(shape).astype(x.dtype)
    x1 = x[..., :half]
    x2 = x[..., half:rot]
    return jnp.concatenate([x1 * cos - x2 * sin, x1 * sin + x2 * cos, x[..., rot:]], axis=-1)

def _query_blocks(fn, qs, pos):
    T = pos.shape[0]
    qb = Q_BLOCK if T % Q_BLOCK == 0 else T
    nb = T // qb
    split = lambda a: jnp.moveaxis(a.reshape((a.shape[0], nb, qb) + a.shape[2:]), 1, 0)
    out = lax.map(lambda args: fn(*args), tuple(split(a) for a in qs) + (pos.reshape(nb, qb),))
    out = jnp.moveaxis(out, 0, 1)
    return out.reshape((out.shape[0], T) + out.shape[3:])

def _chunk_limit(pos_q):
    return (pos_q // CHUNK + 1) * CHUNK

def _dsa_mixer(h, pos, past_k, past_v, past_ki, w_in, w_out):
    Bn, T, _ = h.shape
    q, k, v, qi, ki, wi = jnp.split(h @ w_in, [A_O_Q, A_O_K, A_O_V, A_O_QI, A_O_KI], axis=-1)
    q = _rope(q.reshape(Bn, T, A_HEADS, A_HEAD_DIM), pos, A_ROT)
    k = _rope(k.reshape(Bn, T, A_KV_HEADS, A_HEAD_DIM), pos, A_ROT)
    v = v.reshape(Bn, T, A_KV_HEADS, A_HEAD_DIM)
    qi = _rope(qi.reshape(Bn, T, IDX_HEADS, IDX_DIM), pos, IDX_ROT)
    ki = _rope(ki, pos, IDX_ROT)
    k_all = jnp.concatenate([past_k, k], axis=1)
    v_all = jnp.concatenate([past_v, v], axis=1)
    ki_all = jnp.concatenate([past_ki, ki], axis=1).astype(F32)
    L = k_all.shape[1]
    top = min(TOPK_MAX, L // 4)
    group = A_HEADS // A_KV_HEADS
    scale = A_HEAD_DIM ** -0.5
    iscale = (IDX_HEADS * IDX_DIM) ** -0.5
    key_pos = jnp.arange(L)
    gather = jax.vmap(lambda rows, idx: rows[idx])

    def block(qb, qib, wib, pb):
        n = pb.shape[0]
        dots = jax.nn.relu(jnp.einsum('bthd,bsd->bths', qib.astype(F32), ki_all))
        score = jnp.einsum('bth,bths->bts', wib.astype(F32), dots) * iscale
        limit = _chunk_limit(pb)
        score = jnp.where((key_pos[None, :] < limit[:, None])[None], score, -jnp.inf)
        _, sel = lax.top_k(score, top)
        valid = sel < limit[None, :, None]
        kg = gather(k_all, sel)
        vg = gather(v_all, sel)
        qg = qb.reshape(Bn, n, A_KV_HEADS, group, A_HEAD_DIM)
        logits = jnp.einsum('btkgd,btskd->btkgs', qg, kg).astype(F32) * scale
        logits = jnp.where(valid[:, :, None, None, :], logits, -jnp.inf)
        prob = jax.nn.softmax(logits, axis=-1).astype(vg.dtype)
        o = jnp.einsum('btkgs,btskd->btkgd', prob, vg)
        return o.reshape(Bn, n, A_HEADS * A_HEAD_DIM)

    o = _query_blocks(block, (q, qi, wi), pos)
    return o @ w_out, k, v, ki

def _wkv7_scan(S0, r, decay, k, v, a_vec, b_vec):
    def step(S, inp):
        rt, wt, kt, vt, at, bt = inp
        sa = jnp.einsum('bhij,bhj->bhi', S, at)
        S = S * wt[:, :, None, :] + sa[..., None] * bt[:, :, None, :] + vt[..., None] * kt[:, :, None, :]
        return S, jnp.einsum('bhij,bhj->bhi', S, rt)
    xs = tuple(jnp.moveaxis(t, 1, 0) for t in (r, decay, k, v, a_vec, b_vec))
    S, ys = lax.scan(step, S0, xs)
    return jnp.moveaxis(ys, 0, 1), S

def _rwkv7_mixer(h, shift_prev, S0, mu, w_rkv, w0, w1, w2, a0, a1, a2, g1, g2, k_k, k_a, r_k, ln_w, ln_b, w_out):
    Bn, T, D = h.shape
    h_prev = jnp.concatenate([shift_prev[:, None, :], h[:, :-1]], axis=1)
    xx = h_prev - h
    xm = h[:, :, None, :] + xx[:, :, None, :] * mu
    xr, xw, xk, xv, xa, xg = [xm[:, :, i] for i in range(6)]
    r = xr @ w_rkv[0]
    k = xk @ w_rkv[1]
    v = xv @ w_rkv[2]
    w_log = -jax.nn.softplus(-(w0 + jnp.tanh(xw @ w1) @ w2)) - 0.5
    decay = jnp.exp(-jnp.exp(w_log.astype(F32)))
    a = jax.nn.sigmoid(a0 + (xa @ a1) @ a2)
    g = jax.nn.sigmoid(xg @ g1) @ g2
    hs = lambda t: t.reshape(Bn, T, B_HEADS, B_HEAD_DIM)
    kk = hs(k * k_k).astype(F32)
    kk = kk / jnp.maximum(jnp.sqrt(jnp.sum(kk * kk, axis=-1, keepdims=True)), 1e-12)
    k = k * (1 + (a - 1) * k_a)
    a_h = hs(a).astype(F32)
    y, S = _wkv7_scan(S0.astype(F32), hs(r).astype(F32), hs(decay), hs(k).astype(F32),
                      hs(v).astype(F32), -kk, kk * a_h)
    mean = jnp.mean(y, axis=-1, keepdims=True)
    var = jnp.mean(jnp.square(y - mean), axis=-1, keepdims=True)
    y = ((y - mean) * lax.rsqrt(var + B_GN_EPS)).reshape(Bn, T, D).astype(h.dtype) * ln_w + ln_b
    bonus = jnp.sum(hs(r) * hs(k) * r_k, axis=-1, keepdims=True) * hs(v)
    y = y + bonus.reshape(Bn, T, D)
    return (y * g) @ w_out, h[:, -1], S.astype(h.dtype)

def _mla_mixer(h, pos, past_lat, past_rope, w_in, g_q, g_kv, w_uq, w_ukv, w_out):
    Bn, T, _ = h.shape
    cq, ckv, kpe = jnp.split(h @ w_in, [C_Q_RANK, C_Q_RANK + C_KV_RANK], axis=-1)
    q = (_rmsnorm(cq, g_q) @ w_uq).reshape(Bn, T, C_HEADS, C_NOPE + C_ROPE)
    q_nope = q[..., :C_NOPE]
    q_pe = _rope(q[..., C_NOPE:], pos, C_ROPE)
    lat = _rmsnorm(ckv, g_kv)
    kpe = _rope(kpe, pos, C_ROPE)
    lat_all = jnp.concatenate([past_lat, lat], axis=1)
    kpe_all = jnp.concatenate([past_rope, kpe], axis=1)
    L = lat_all.shape[1]
    kv = (lat_all @ w_ukv).reshape(Bn, L, C_HEADS, C_NOPE + C_V)
    k_nope = kv[..., :C_NOPE]
    v = kv[..., C_NOPE:]
    scale = (C_NOPE + C_ROPE) ** -0.5
    key_pos = jnp.arange(L)

    def block(qn, qp, pb):
        logits = (jnp.einsum('bthd,bshd->bhts', qn, k_nope)
                  + jnp.einsum('bthr,bsr->bhts', qp, kpe_all)).astype(F32) * scale
        adm = key_pos[None, :] < _chunk_limit(pb)[:, None]
        logits = jnp.where(adm[None, None], logits, -jnp.inf)
        prob = jax.nn.softmax(logits, axis=-1).astype(v.dtype)
        return jnp.einsum('bhts,bshd->bthd', prob, v).reshape(Bn, pb.shape[0], C_HEADS * C_V)

    o = _query_blocks(block, (q_nope, q_pe), pos)
    return o @ w_out, lat, kpe

def _conv_ffn(h, conv_prev, w_up, w_conv, b_conv, w_down):
    T = h.shape[1]
    u = h @ w_up
    u_pad = jnp.concatenate([conv_prev, u], axis=1)
    c = b_conv + sum(u_pad[:, j:j + T] * w_conv[j] for j in range(CONV_W))
    gate, val = jnp.split(c, 2, axis=-1)
    return (jax.nn.silu(gate) * val) @ w_down, u_pad[:, T:]

def _trunk(x, pos, st, w):
    new = {name: [] for name in ('a_k', 'a_v', 'a_idx', 'b_wkv', 'b_shift', 'c_lat', 'c_rope', 'ffn')}
    for i in range(DEPTH):
        j = i // N_MIXERS
        kind = i % N_MIXERS
        hn = _rmsnorm(x, w['n_mix'][i])
        if kind == 0:
            out, k, v, ki = _dsa_mixer(hn, pos, st['a_k'][j], st['a_v'][j], st['a_idx'][j],
                                       w['a_w_in'][j], w['a_w_out'][j])
            new['a_k'].append(k)
            new['a_v'].append(v)
            new['a_idx'].append(ki)
        elif kind == 1:
            out, shift, S = _rwkv7_mixer(hn, st['b_shift'][j], st['b_wkv'][j], w['b_mu'][j], w['b_w_rkv'][j],
                                         w['b_w0'][j], w['b_w1'][j], w['b_w2'][j], w['b_a0'][j], w['b_a1'][j],
                                         w['b_a2'][j], w['b_g1'][j], w['b_g2'][j], w['b_k_k'][j], w['b_k_a'][j],
                                         w['b_r_k'][j], w['b_ln_w'][j], w['b_ln_b'][j], w['b_w_out'][j])
            new['b_shift'].append(shift)
            new['b_wkv'].append(S)
        else:
            out, lat, kpe = _mla_mixer(hn, pos, st['c_lat'][j], st['c_rope'][j], w['c_w_in'][j], w['c_g_q'][j],
                                       w['c_g_kv'][j], w['c_w_uq'][j], w['c_w_ukv'][j], w['c_w_out'][j])
            new['c_lat'].append(lat)
            new['c_rope'].append(kpe)
        x = x + out
        out, cbuf = _conv_ffn(_rmsnorm(x, w['n_ffn'][i]), st['ffn'][i], w['f_w_up'][i], w['f_w_conv'][i],
                              w['f_b_conv'][i], w['f_w_down'][i])
        new['ffn'].append(cbuf)
        x = x + out
    y = _rmsnorm(x, w['n_final'])
    return y, {name: jnp.stack(rows, axis=0) for name, rows in new.items()}

def setup_inputs(seed: int = 0) -> dict:
    key = jax.random.key(seed)
    ks = list(jax.random.split(key, 48))

    def nrm(shape, scale):
        return jax.random.normal(ks.pop(), shape, F32) * scale

    def unif(shape, lo, hi):
        return jax.random.uniform(ks.pop(), shape, F32, lo, hi)

    D = D_MODEL
    F2 = 2 * D_FF
    return {
        'x_prompt': nrm((BATCH, SEQ, D), 1.0),
        'x_sample': nrm((DEC_BATCH, DEC_SEQ, D), 1.0),
        'cache_a_k': nrm((N_A, DEC_BATCH, PAST_LEN, A_KV_HEADS, A_HEAD_DIM), 1.0),
        'cache_a_v': nrm((N_A, DEC_BATCH, PAST_LEN, A_KV_HEADS, A_HEAD_DIM), 1.0),
        'cache_a_idx': nrm((N_A, DEC_BATCH, PAST_LEN, IDX_DIM), 1.0),
        'state_b_wkv': nrm((N_B, DEC_BATCH, B_HEADS, B_HEAD_DIM, B_HEAD_DIM), 0.1),
        'state_b_shift': nrm((N_B, DEC_BATCH, D), 1.0),
        'cache_c_latent': nrm((N_C, DEC_BATCH, PAST_LEN, C_KV_RANK), 1.0),
        'cache_c_rope': nrm((N_C, DEC_BATCH, PAST_LEN, C_ROPE), 1.0),
        'state_ffn_conv': nrm((DEPTH, DEC_BATCH, CONV_W - 1, F2), 1.0),
        'n_mix': 1.0 + nrm((DEPTH, D), 0.02),
        'n_ffn': 1.0 + nrm((DEPTH, D), 0.02),
        'n_final': 1.0 + nrm((D,), 0.02),
        'a_w_in': nrm((N_A, D, A_IN), D ** -0.5),
        'a_w_out': nrm((N_A, A_HEADS * A_HEAD_DIM, D), (A_HEADS * A_HEAD_DIM) ** -0.5),
        'b_mu': unif((N_B, 6, D), 0.0, 1.0),
        'b_w_rkv': nrm((N_B, 3, D, D), D ** -0.5),
        'b_w0': unif((N_B, D), -5.0, 1.0),
        'b_w1': nrm((N_B, D, B_DECAY_LORA), D ** -0.5),
        'b_w2': nrm((N_B, B_DECAY_LORA, D), 0.1 * B_DECAY_LORA ** -0.5),
        'b_a0': nrm((N_B, D), 0.1),
        'b_a1': nrm((N_B, D, B_ICL_LORA), D ** -0.5),
        'b_a2': nrm((N_B, B_ICL_LORA, D), 0.1 * B_ICL_LORA ** -0.5),
        'b_g1': nrm((N_B, D, B_GATE_LORA), D ** -0.5),
        'b_g2': nrm((N_B, B_GATE_LORA, D), B_GATE_LORA ** -0.5),
        'b_k_k': 0.85 + nrm((N_B, D), 0.02),
        'b_k_a': 1.0 + nrm((N_B, D), 0.02),
        'b_r_k': nrm((N_B, B_HEADS, B_HEAD_DIM), 0.1),
        'b_ln_w': 1.0 + nrm((N_B, D), 0.02),
        'b_ln_b': nrm((N_B, D), 0.01),
        'b_w_out': nrm((N_B, D, D), D ** -0.5),
        'c_w_in': nrm((N_C, D, C_IN), D ** -0.5),
        'c_g_q': 1.0 + nrm((N_C, C_Q_RANK), 0.02),
        'c_g_kv': 1.0 + nrm((N_C, C_KV_RANK), 0.02),
        'c_w_uq': nrm((N_C, C_Q_RANK, C_HEADS * (C_NOPE + C_ROPE)), C_Q_RANK ** -0.5),
        'c_w_ukv': nrm((N_C, C_KV_RANK, C_HEADS * (C_NOPE + C_V)), C_KV_RANK ** -0.5),
        'c_w_out': nrm((N_C, C_HEADS * C_V, D), (C_HEADS * C_V) ** -0.5),
        'f_w_up': nrm((DEPTH, D, F2), D ** -0.5),
        'f_w_conv': nrm((DEPTH, CONV_W, F2), CONV_W ** -0.5),
        'f_b_conv': nrm((DEPTH, F2), 0.01),
        'f_w_down': nrm((DEPTH, D_FF, D), D_FF ** -0.5),
    }

def reference(x_prompt, x_sample, cache_a_k, cache_a_v, cache_a_idx, state_b_wkv, state_b_shift,
              cache_c_latent, cache_c_rope, state_ffn_conv, n_mix, n_ffn, n_final, a_w_in, a_w_out,
              b_mu, b_w_rkv, b_w0, b_w1, b_w2, b_a0, b_a1, b_a2, b_g1, b_g2, b_k_k, b_k_a, b_r_k,
              b_ln_w, b_ln_b, b_w_out, c_w_in, c_g_q, c_g_kv, c_w_uq, c_w_ukv, c_w_out,
              f_w_up, f_w_conv, f_b_conv, f_w_down):
    w = dict(n_mix=n_mix, n_ffn=n_ffn, n_final=n_final, a_w_in=a_w_in, a_w_out=a_w_out,
             b_mu=b_mu, b_w_rkv=b_w_rkv, b_w0=b_w0, b_w1=b_w1, b_w2=b_w2, b_a0=b_a0, b_a1=b_a1,
             b_a2=b_a2, b_g1=b_g1, b_g2=b_g2, b_k_k=b_k_k, b_k_a=b_k_a, b_r_k=b_r_k,
             b_ln_w=b_ln_w, b_ln_b=b_ln_b, b_w_out=b_w_out, c_w_in=c_w_in, c_g_q=c_g_q,
             c_g_kv=c_g_kv, c_w_uq=c_w_uq, c_w_ukv=c_w_ukv, c_w_out=c_w_out,
             f_w_up=f_w_up, f_w_conv=f_w_conv, f_b_conv=f_b_conv, f_w_down=f_w_down)
    Bp, Tp, D = x_prompt.shape
    dt = x_prompt.dtype
    st_prompt = dict(
        a_k=jnp.zeros((N_A, Bp, 0, A_KV_HEADS, A_HEAD_DIM), dt),
        a_v=jnp.zeros((N_A, Bp, 0, A_KV_HEADS, A_HEAD_DIM), dt),
        a_idx=jnp.zeros((N_A, Bp, 0, IDX_DIM), dt),
        b_wkv=jnp.zeros((N_B, Bp, B_HEADS, B_HEAD_DIM, B_HEAD_DIM), dt),
        b_shift=jnp.zeros((N_B, Bp, D), dt),
        c_lat=jnp.zeros((N_C, Bp, 0, C_KV_RANK), dt),
        c_rope=jnp.zeros((N_C, Bp, 0, C_ROPE), dt),
        ffn=jnp.zeros((DEPTH, Bp, CONV_W - 1, 2 * D_FF), dt))
    st_sample = dict(a_k=cache_a_k, a_v=cache_a_v, a_idx=cache_a_idx, b_wkv=state_b_wkv,
                     b_shift=state_b_shift, c_lat=cache_c_latent, c_rope=cache_c_rope,
                     ffn=state_ffn_conv)
    pos_prompt = jnp.arange(Tp, dtype=jnp.int32)
    pos_sample = cache_a_k.shape[2] + jnp.arange(x_sample.shape[1], dtype=jnp.int32)
    y_prompt, sp = _trunk(x_prompt, pos_prompt, st_prompt, w)
    y_sample, ss = _trunk(x_sample, pos_sample, st_sample, w)
    return (y_prompt, y_sample,
            sp['a_k'], ss['a_k'], sp['a_v'], ss['a_v'], sp['a_idx'], ss['a_idx'],
            sp['b_wkv'], ss['b_wkv'], sp['b_shift'], ss['b_shift'],
            sp['c_lat'], ss['c_lat'], sp['c_rope'], ss['c_rope'],
            sp['ffn'], ss['ffn'])


_drawn_inputs = setup_inputs


def setup_inputs(seed=0):
    import zlib

    import numpy as np

    out = dict(_drawn_inputs(seed))
    spreads = {}
    factors = {'n_final': 2.942,
     'b_w1': 6.067,
     'b_w2': 6.168,
     'b_k_k': 3.574,
     'b_ln_w': 2.688,
     'b_ln_b': 4.655,
     'c_g_q': 7.336,
     'c_g_kv': 2.909}
    for name, (base, spread) in spreads.items():
        noise = np.random.default_rng([zlib.crc32(name.encode()), seed]).standard_normal(out[name].shape)
        drawn = base * np.exp(spread * noise) if base else spread * noise
        out[name] = __import__('jax').numpy.asarray(drawn.astype(out[name].dtype))
    for name, factor in factors.items():
        out[name] = (out[name] * factor).astype(out[name].dtype)
    return out
```

```python
from contextlib import ExitStack

import numpy as np

import concourse.bass as bass
from concourse import mybir

F32 = mybir.dt.float32
F32R = mybir.dt.float32r
ALU = mybir.AluOpType
ACT = mybir.ActivationFunctionType


D, KD = 1024, 8
SEQ, DEC, PAST = 256, 64, 128
T = DEC + SEQ
KEYS = PAST + T
DEPTH, DFF = 4, 2816
NF = DFF // 128
TG = T + 2
EPS = 1e-6
PAIRS = 8
EARLY = 3
SLOT = 2304
CHUNK = 64
REPLACED, INVALID, OFF = -3.3e38, -2.0e38, -1e30
A_SCALE, I_SCALE, C_SCALE = 64 ** -0.5, 512 ** -0.5, 96 ** -0.5
DECAY = -float(np.exp(np.float32(-0.5)))

VECS = [("f_w_conv", 4 * 3 * 44), ("f_b_conv", 4 * 44), ("state_ffn_conv", 4 * 2 * 44), ("n_mix", 32), ("n_ffn", 32),
        ("n_final", 8), ("b_mu", 48), ("b_w0", 8), ("b_a0", 8), ("b_k_k", 8), ("b_k_a", 8), ("b_r_k", 8),
        ("b_ln_w", 8), ("b_ln_b", 8), ("state_b_shift", 8), ("c_g_q", 4), ("c_g_kv", 2)]
VOFF, _n = {}, 0
for _name, _rows in VECS:
    VOFF[_name] = _n
    _n += _rows
NVEC = _n
VGROUPS = -(-NVEC // 128)

CONSTS = [("ident", 128), ("ones", 128), ("headsum", 128), ("perm_a", 128), ("perm_c", 96), ("place", 96),
          ("place_rot", 96), ("cos_a", T), ("sin_a", T), ("cos_c", T), ("sin_c", T), ("valid0", 128),
          ("valid1", 256), ("off0", 128), ("off1", 256), ("m_diag", 128), ("mt_diag", 128), ("m_off", 128),
          ("mt_strict", 128), ("mt_incl", 64), ("scan_keep", T), ("zero", 192), ("eps", 3)]
COFF, _n = {}, 0
for _name, _w in CONSTS:
    COFF[_name] = (_n, _w)
    _n += _w
NCONST = _n


def constants():
    c = np.zeros((128, NCONST), np.float32)

    def put(name, a):
        o, w = COFF[name]
        c[:a.shape[0], o:o + w] = a

    put("ident", np.eye(128))
    put("ones", np.ones((128, 128)))
    h = np.arange(128) // 64
    put("headsum", (h[:, None] == h[None, :]).astype(np.float32))
    pos = np.concatenate([PAST + np.arange(DEC), np.arange(SEQ)]).astype(np.float32)

    def tables(rot):
        half = rot // 2
        inv = np.float32(500000.0) ** (-np.arange(half, dtype=np.float32) / np.float32(half))
        ang = (pos[:, None] * inv[None, :]).astype(np.float32)
        return np.cos(ang).T, np.sin(ang).T

    def rotate(rot, base, n, m):
        p = np.zeros((n, m), np.float32)
        half = rot // 2
        for b in base:
            for i in range(half):
                p[b + i + half, b + i] = -1.0
                p[b + i, b + i + half] = 1.0
        return p

    put("perm_a", rotate(16, (0, 64), 128, 128))
    put("perm_c", rotate(32, (64,), 96, 96))
    place = np.zeros((128, 96), np.float32)
    place[96 + np.arange(32), 64 + np.arange(32)] = 1.0
    put("place", place)
    rot = rotate(32, (64,), 96, 96)
    placed = np.zeros((128, 96), np.float32)
    placed[96:128] = rot[64:96]
    put("place_rot", placed)
    cos, sin = tables(16)
    ca, sa = np.ones((128, T), np.float32), np.zeros((128, T), np.float32)
    for b in (0, 64):
        ca[b:b + 8], ca[b + 8:b + 16] = cos, cos
        sa[b:b + 8], sa[b + 8:b + 16] = sin, sin
    put("cos_a", ca)
    put("sin_a", sa)
    cos, sin = tables(32)
    cc, sc = np.ones((96, T), np.float32), np.zeros((96, T), np.float32)
    cc[64:80], cc[80:96], sc[64:80], sc[80:96] = cos, cos, sin, sin
    put("cos_c", cc)
    put("sin_c", sc)
    q = np.arange(128)
    in0 = np.arange(128)[None, :] < ((q // 64 + 1) * 64)[:, None]
    in1 = np.arange(256)[None, :] < (((q + 128) // 64 + 1) * 64)[:, None]
    put("valid0", np.where(in0, 0.0, INVALID))
    put("valid1", np.where(in1, 0.0, INVALID))
    put("off0", np.where(in0, 0.0, OFF))
    put("off1", np.where(in1, 0.0, OFF))
    same = h[:, None] == h[None, :]
    r, s = np.arange(128)[:, None], np.arange(128)[None, :]
    sub = (r // 16) == (s // 16)
    put("m_diag", (same & sub & (s < r)).astype(np.float32))
    put("m_off", (same & ~sub & (s < r)).astype(np.float32))
    put("mt_diag", (same & sub & (r < s)).astype(np.float32))
    put("mt_strict", (same & (r < s)).astype(np.float32))
    put("mt_incl", ((r % 64) <= np.arange(64)[None, :]).astype(np.float32))
    keep = np.ones((128, T), np.float32)
    keep[:, ::CHUNK] = 0.0
    put("scan_keep", keep)
    put("eps", np.broadcast_to(np.array([EPS, 64e-5, 0.0], np.float32), (128, 3)))
    return c


class Slab:

    def __init__(self, kind, idx, kt, w, loads, chunks):
        self.kind, self.idx, self.kt, self.w, self.loads, self.chunks = kind, idx, kt, w, loads, chunks
        self.layer = None


def vec_rows(ap):
    names = "abcdef"[:len(ap.shape)]
    flat = ap if len(ap.shape) == 1 else ap.rearrange(f"{' '.join(names)} -> ({' '.join(names)})")
    return flat.rearrange("(r q) -> r q", q=128)


UNITS = ((0, 128), (128, 384), (384, 512), (512, 768), (768, 960))


def build(nc, i_, o_):
    slabs, first_slab = [], {}

    def begin(key):
        first_slab[key] = len(slabs)

    def cols(w, c0, n, k0=0, kt=None):
        kt = kt or w.shape[0] // 128
        return w[k0 * 128:(k0 + kt) * 128, c0:c0 + n].rearrange("(k p) n -> p k n", p=128)

    def plain(kind, key, w, n_cols, width, chunks, kt):
        begin((key, kind))
        for j in range(n_cols // width):
            slabs.append(Slab(kind, j, kt, width, [(0, cols(w, j * width, width))], chunks))

    for layer in range(DEPTH):
        mixer, inst = layer % 3, layer // 3
        start = len(slabs)
        if mixer == 0:
            w = i_["a_w_in"][inst]
            begin((layer, "mix"))
            k, v, ki, wi = 1024, 1152, 1792, 1856
            slabs.append(Slab("kk", 0, 8, 264, [(0, cols(w, k, 64)), (64, cols(w, k, 64)), (128, cols(w, k + 64, 64)),
                                                (192, cols(w, k + 64, 64)), (256, cols(w, wi, 8))], 3))
            slabs.append(Slab("kiv", 0, 8, 256, [(0, cols(w, ki, 64)), (64, cols(w, ki, 64)), (128, cols(w, v, 128))], 2))
            for j in range(2):
                slabs.append(Slab("qi", j, 8, 256, [(0, cols(w, 1280 + 256 * j, 256))], 2))
            for j in range(4):
                slabs.append(Slab("q", j, 8, 256, [(0, cols(w, 256 * j, 256))], 2))
            plain("out", layer, i_["a_w_out"][inst], D, 256, 2, 8)
        elif mixer == 1:
            begin((layer, "mix"))
            for m in range(3):
                for j in range(4):
                    slabs.append(Slab("rkv", m, 8, 256, [(0, cols(i_["b_w_rkv"][inst, m], 256 * j, 256))], 2))
            plain("out", layer, i_["b_w_out"][inst], D, 256, 2, 8)
        else:
            w = i_["c_w_in"][inst]
            begin((layer, "mix"))
            for j in range(2):
                slabs.append(Slab("cq", j, 8, 256, [(0, cols(w, 256 * j, 256))], 2))
            slabs.append(Slab("ckv", 0, 8, 288, [(0, cols(w, 512, 288))], 3))
            for j in range(2):
                slabs.append(Slab("ukv", j, 2, 1024, [(0, cols(i_["c_w_ukv"][inst], 1024 * j, 1024))], 12))
            for j in range(4):
                slabs.append(Slab("uq", j, 4, 384, [(0, cols(i_["c_w_uq"][inst], 384 * j, 384))], 4))
            plain("out", layer, i_["c_w_out"][inst], D, 256, 2, 8)
        w = i_["f_w_up"][layer]
        begin((layer, "up"))
        for f in range(NF):
            slabs.append(Slab("up", f, 8, 256, [(0, cols(w, f * 128, 128)), (128, cols(w, DFF + f * 128, 128))], 2))
        w = i_["f_w_down"][layer]
        begin((layer, "down"))
        for m in range(KD):
            for half in range(2):
                slabs.append(Slab("down", m, 11, 128, [(0, cols(w, m * 128, 128, 11 * half, 11))], 1))
        for s in slabs[start:]:
            s.layer = layer
    N = len(slabs)
    done_after, raw_after, c, r = [], [], 0, [0, 0]
    for n, s in enumerate(slabs):
        c += s.chunks
        r[n % 2] += 16 * len(s.loads)
        done_after.append(c)
        raw_after.append(r[n % 2])

    with ExitStack() as ctx:
        base = [-(-nc.sbuf_base // 64) * 64]

        def at(name, shape, dt, offset):
            return nc.alloc_sbuf_tensor_at(name, shape, dt, offset=offset)

        def size(shape):
            b = 4
            for x in shape[1:]:
                b *= x
            return -(-b // 64) * 64

        def sb(name, shape, dt=F32):
            t = at(name, shape, dt, base[0])
            base[0] += size(shape)
            return t

        def sem(name):
            return ctx.enter_context(nc.semaphore(name))

        xT = sb("xT", [128, KD, T])
        con = sb("con", [128, NCONST])
        V = sb("V", [128, VGROUPS * 128])
        raw_at = base[0]
        raw = [sb(f"raw{j}", [128, SLOT]) for j in range(2)]
        hi = [sb(f"hi{j}", [128, SLOT], F32R) for j in range(2)]
        lo = [sb(f"lo{j}", [128, SLOT], F32R) for j in range(2)]
        x_at = base[0]
        XH = sb("XH", [128, KD, T], F32R)
        XL = sb("XL", [128, KD, T], F32R)
        sq_at = base[0]
        sq = sb("sq", [128, 2, T])
        ssq = sb("ssq", [128, T])
        rms_at = base[0]
        rms = sb("rms", [128, T])
        rstd = sb("rstd", [128, T])
        xn = sb("xn", [128, 2, T])
        uout = sb("uout", [128, 2, 128])
        over = base[0]
        limit = nc.sbuf_usable_end

        def region(start):
            pos = [start]

            def take(name, shape, dt=F32):
                t = at(name, shape, dt, pos[0])
                pos[0] += size(shape)
                assert pos[0] <= limit, (name, pos[0], limit)
                return t
            return take

        def C(name, rows=128):
            o, w = COFF[name]
            return con[0:rows, o:o + w]

        def vcol(name, j):
            return V[:, VOFF[name] + j:VOFF[name] + j + 1]

        take = region(over)
        vrows = take("vrows", [128, VGROUPS, 128])
        xin = take("xin", [128, 3, D])
        take = region(over)
        GH = take("GH", [128, NF, TG], F32R)
        GL = take("GL", [128, NF, TG], F32R)
        upad = take("upad", [128, 2, 2, TG + 2])
        conv = take("conv", [128, 2, 2, TG])
        silu = take("silu", [128, TG])
        gated = take("gated", [128, TG])
        ust = take("ust", [128, 2, 2, 2 * NF])
        take = region(over)
        OH = take("OH", [128, KD, T], F32R)
        OL = take("OL", [128, KD, T], F32R)
        QT = take("QT", [128, 2, 2, T])
        LS2 = take("LS2", [128, 2, 960])
        negmax = take("negmax", [128, 3, 8])
        sums = take("sums", [128, 3, 8])
        rsum = take("rsum", [128, 3, 8])
        PT = take("PT", [128, 1024])
        qraw = take("qraw", [128, 2, T])
        qcos = take("qcos", [128, 2, T])
        qsin = take("qsin", [128, T])
        attn_end = over + 2 * size([128, KD, T]) + size([128, 2, 2, T]) + size([128, 2, 960]) + 3 * size([128, 3, 8]) + \
            size([128, 1024]) + 2 * size([128, 2, T]) + size([128, T])
        take = region(attn_end)
        KT = take("KT", [128, 2, KEYS])
        KIT = take("KIT", [128, KEYS])
        QIT = take("QIT", [128, 4, T])
        VTf = take("VTf", [128, T])
        WIf = take("WIf", [128, T])
        ck = take("ck", [128, 2, 2, 64])
        ci = take("ci", [128, 2, 64])
        Vc = take("Vc", [128, 128])
        Vt = take("Vt", [128, 3, 128])
        Ko = take("Ko", [128, 3, 128])
        KIo = take("KIo", [128, 3, 64])
        WI = take("WI", [128, 3, 8])
        relu = take("relu", [128, 2, 576])
        SC = take("SC", [128, 576])
        SW = take("SW", [128, 576])
        MK = take("MK", [128, 576])
        top8 = take("top8", [128, 3, 8])
        LS3 = take("LS3", [128, 960])

        def slot(q):
            return q % (2 if PAIRS <= q < 2 * PAIRS else 3)

        def LS(q):
            return LS3[:, :] if slot(q) == 2 else LS2[:, slot(q), :]

        QD = take("QD", [128, PAIRS, T])
        cosr = take("cosr", [128, T])
        sinr = take("sinr", [128, T])
        take = region(attn_end)
        KC = take("KC", [96, 16, KEYS])
        VC = take("VC", [128, 4, D])
        KPE = take("KPE", [96, T])
        lato = take("lato", [128, 3, 256])
        ropeo = take("ropeo", [128, 3, 96])
        take = region(over)
        CQ = take("CQ", [128, 6, T])
        LATF = take("LATF", [128, 2, KEYS])
        cr = take("cr", [128, 96])
        cl = take("cl", [128, 256])
        XHf, XLf = (t[:].rearrange("p k n -> p (k n)") for t in (XH, XL))
        LATH, LATL = (t[:, 4 * T:4 * T + 2 * KEYS].rearrange("p (k n) -> p k n", k=2) for t in (XHf, XLf))
        take = region(over)
        HN = take("HN", [128, KD, T])
        XX = take("XX", [128, KD, T])
        MX = take("MX", [128, KD, T])
        R = take("R", [128, KD, T])
        K = take("K", [128, KD, T])
        VV = take("VV", [128, KD, T])
        LW = take("LW", [128, KD, T])
        A = take("A", [128, KD, T])
        G = take("G", [128, KD, T])
        LT = take("LT", [128, T])
        LTg = at("LTg", [128, T], F32, rms_at)
        Dend = take("Dend", [128, KD, 5])
        onemka = take("onemka", [128, KD])
        sho = take("sho", [128, 16])
        shot = take("shot", [16, 128])
        x_take = region(x_at)
        L1 = x_take("L1", [128, KD, 256])
        L2 = x_take("L2", [128, 2, D])
        SS = [at(f"SS{g}", [128, 4, 128], F32, a_) for g, a_ in enumerate((sq_at, rms_at))]
        x_take = region(x_at)
        T1 = x_take("T1", [128, KD, T])
        T2 = x_take("T2", [128, KD, T])
        slots_ = []
        for nm, a0, cnt in (("HN", over, 5), ("LW", over + 6 * size([128, KD, T]), 5), ("T1", x_at, 5), ("T2", x_at + size([128, KD, T]), 5)):
            slots_ += [a0 + 2048 * z for z in range(cnt)]
        BD = [[at(f"bd{g}_{z}", [128, 4, 128], F32, slots_[g * 10 + z]) for z in range(10)] for g in range(2)]
        BX = [[at(f"bx{g}_{z}", [128, 4, 128], F32, raw_at + 2048 * (g * 4 + z)) for z in range(4)] for g in range(2)]
        psum = [ctx.enter_context(nc.psum_tensor(f"bank{b}", [128, 512], F32)) for b in range(8)]

        w_raw = [sem("w_raw0"), sem("w_raw1")]
        (w_hi, w_lo, mm_done, con_in, vec_in, x_in, cache_in, stored) = map(
            sem, "w_hi w_lo mm_done con_in vec_in x_in cache_in stored".split())
        (vt_ready, v_copied, xt_ready, x_done, sq_done, ssq_done, ms_done, rms_done, xn_done) = map(
            sem, "vt_ready v_copied xt_ready x_done sq_done ssq_done ms_done rms_done xn_done".split())
        (u_evac, c2_done, hist_done, ust_done, ffn_step, silu_done, g_done, ust_turned, ust_copied) = map(
            sem, "u_evac c2_done hist_done ust_done ffn_step silu_done g_done ust_turned ust_copied".split())
        (tile_evac, perm_done, cos_done, rope_done, turned, turned_in, rows_out, dots_done, relu_done, score_done,
         mask_done, mask_copied) = map(sem, ("tile_evac perm_done cos_done rope_done turned turned_in rows_out dots_done "
                                             "relu_done score_done mask_done mask_copied").split())
        (qk_done, max_done, exp_done, prob_done, pt_turned, pt_act, pt_dve, pv_done, oh_done, ol_done) = map(
            sem, "qk_done max_done exp_done prob_done pt_turned pt_act pt_dve pv_done oh_done ol_done".split())
        rows_turned = sem("rows_turned")
        (dve_c, act_c, pool_c, pads_set, y_turned, y_copied, xh_done, rstd_done, u_raw, cosr_done, rows_scaled) = map(
            sem, "dve_c act_c pool_c pads_set y_turned y_copied xh_done rstd_done u_raw cosr_done rows_scaled".split())

        NORMS = [("in", 8)]
        for layer in range(DEPTH):
            if layer % 3 == 2:
                NORMS += [("cq", 4), ("ckv", 2)]
            NORMS += [("mid", 8), ("end", 8)]
        norm_base = np.cumsum([0] + [n for _, n in NORMS]).tolist()
        norm_of, k_ = {}, 1
        for layer in range(DEPTH):
            norm_of[layer, "mix"] = k_ - 1
            if layer % 3 == 2:
                norm_of[layer, "cq"], norm_of[layer, "ckv"] = k_, k_ + 1
                k_ += 2
            norm_of[layer, "ffn"] = k_
            k_ += 2
        norm_final = k_ - 1
        x_norms = [j for j, (_, n) in enumerate(NORMS) if n == 8]
        xs_of = {j: s for s, j in enumerate(x_norms)}

        class Chain:

            def __init__(self, eng, s):
                self.eng, self.s, self.n = eng, s, 0

            def __call__(self, ins):
                ins.then_inc(self.s, 1)
                self.n += 1
                self.eng.wait_ge(self.s, self.n)

        def gain(j, k):
            name, layer = j
            return vcol(name, layer * 8 + k if name != "n_final" else k)

        GAIN = {}
        for layer in range(DEPTH):
            GAIN[norm_of[layer, "mix"]] = ("n_mix", layer)
            GAIN[norm_of[layer, "ffn"]] = ("n_ffn", layer)
        GAIN[norm_final] = ("n_final", 0)
        TILES = ((0, 64), (64, 128), (192, 128))

        (mix_done, rkv_evac, lora_in, lora_mid, lora_act, lora_out, lora_evac, shift_set, shift_turned, shift_out) = map(
            sem, "mix_done rkv_evac lora_in lora_mid lora_act lora_out lora_evac shift_set shift_turned shift_out".split())
        (lw_done, cc_done, decay_done, lwp_done, prev_done, kk_raw, kk_sq, hs_done, hs_root, bonus_in, bonus_out, rec_ready) = map(
            sem, "lw_done cc_done decay_done lwp_done prev_done kk_raw kk_sq hs_done hs_root bonus_in bonus_out rec_ready".split())
        (built_pool, built_dve, state_in, state_turned, state_set, z_turned, z_staged, rec_done, y_mean, y_sq, y_root, y_parts) = map(
            sem, "built_pool built_dve state_in state_turned state_set z_turned z_staged rec_done y_mean y_sq y_root y_parts".split())
        state_stored, y_inv, y_gated = sem("state_stored"), sem("y_inv"), sem("y_gated")
        (placed, cqn_done, lat_parts, mla_turned, mla_cached, kc_rope, latf_done) = map(
            sem, "placed cqn_done lat_parts mla_turned mla_cached kc_rope latf_done".split())
        stage_pe = [sem("stage_pe0"), sem("stage_pe1")]
        stage_act = [sem("stage_act0"), sem("stage_act1")]
        stage_dve = [sem("stage_dve0"), sem("stage_dve1")]

        STAGES = [("mT", "d", ()), ("m", "d", ()), ("nT", "d", ()), ("arT", "d", ()),
                  ("vt", "a", (0,)), ("bt", "a", (1,)), ("kt", "a", (2,)),
                  ("m2", "a", (0, 1, 3)), ("m2T", "a", (0, 1, 4)), ("p2", "d", (7, 0, 5)),
                  ("m4", "a", (7, 8, 6)), ("m4T", "a", (7, 8)), ("p4", "d", (10, 9, 8)),
                  ("m8", "a", (10, 11, 9)), ("p8", "d", (13, 12, 10)), ("qT", "ad", (14, 1, 11)),
                  ("q", "a", (14, 1, 12)), ("q2", "a", (15, 16, 13)), ("h", "d", (17, 15, 14)),
                  ("rhs", "a", (4, 2, 15)), ("x1", "a", (19, 14, 16)), ("u", "a", (20, 18, 17)),
                  ("y", "a", (21, 3, 18)), ("z", "d", (21, 6, 5, 19))]
        ACT_AT, DVE_AT, a_, d_ = {}, {}, 0, 0
        for z_, (_, e_, _) in enumerate(STAGES):
            if "a" in e_:
                a_ += 1
                ACT_AT[z_] = a_
            if "d" in e_:
                d_ += 1
                DVE_AT[z_] = d_
        ACT_STAGES, DVE_STAGES = a_, d_
        CHUNKS = 5

        def taken(eng, g, c, z):
            if z in ACT_AT:
                eng.wait_ge(stage_act[g], c * ACT_STAGES + ACT_AT[z])
            if z in DVE_AT:
                eng.wait_ge(stage_dve[g], c * DVE_STAGES + DVE_AT[z])

        vec_loads = [0]
        STORES_AT = {}
        block = ctx.enter_context(nc.Block())

        @block.sync
        def _(sp):
            sp.dma_start(con[:, :], i_["const"]).then_inc(con_in, 16)
            xs, xp = i_["x_sample"][0], i_["x_prompt"][0]
            sp.dma_start(xin[0:64, 0, :], xs).then_inc(x_in, 16)
            sp.dma_start(xin[:, 1, :], xp[0:128]).then_inc(x_in, 16)
            sp.dma_start(xin[:, 2, :], xp[128:256]).then_inc(x_in, 16)

            def load(n, f=None, i=None):
                s = slabs[n]
                for dst, src in s.loads:
                    sp.dma_start(raw[n % 2][:, 0:s.kt * s.w].rearrange("p (k w) -> p k w", w=s.w)[:, :, dst:dst + src.shape[2]],
                                 src).then_inc(w_raw[n % 2], 16)

            def wait_free(n):
                if not isinstance(n, int) or n >= 2:
                    sp.wait_ge(w_hi, n - 1)
                    sp.wait_ge(w_lo, n - 1)

            n = 0
            while n < N:
                s = slabs[n]
                if s.kind == "up":
                    layer = s.layer
                    w = i_["f_w_up"][layer]
                    with sp.Fori(0, NF // 2) as i:
                        for j in range(2):
                            wait_free(i * 2 + (n + j))
                            dst = raw[(n + j) % 2][:, 0:2048].rearrange("p (k w) -> p k w", w=256)
                            for h in range(2):
                                src = w[:, bass.ds((i * 2 + j) * 128 + h * DFF, 128)].rearrange("(k p) n -> p k n", p=128)
                                sp.dma_start(dst[:, :, h * 128:h * 128 + 128], src).then_inc(w_raw[(n + j) % 2], 16)
                    n += NF
                else:
                    wait_free(n)
                    if s.kind == "out" and s.layer == 1 and s.idx < 2:
                        sp.wait_ge(rec_done, 1)
                    load(n)
                    n += 1

        A_ROPE = (0, 1, 3, 5, 6, 7, 8, 9, 10, 11, 12, 13, 14, 15, 16)
        R0, E0, Q0, ROWS_BEFORE = {}, {}, {}, {}
        r_, e_, q_, w_ = 0, 0, 0, 0
        for layer in range(DEPTH):
            R0[layer], E0[layer], Q0[layer], ROWS_BEFORE[layer] = r_, e_, q_, w_
            mixer = layer % 3
            r_ += (15, 0, 17)[mixer]
            e_ += (17, 0, 7 + 8 + 16 + 16)[mixer]
            q_ += (8, 0, 8)[mixer]
            w_ += (3, 0, 3)[mixer]

        CACHE_LOADS = {0: 7, 2: 7 + 2, 3: 7 + 2 + 7}
        XN = {j: 8 * z for z, j in enumerate(j for j in x_norms if j != norm_of[1, "mix"])}

        def norm_next(layer):
            return norm_of[layer + 1, "mix"] if layer + 1 < DEPTH else norm_final

        LATE = {j for j in XN if j != norm_final}

        @block.gpsimd
        def _(pool):
            chain = Chain(pool, pool_c)
            stores = [0]

            def store(dst, src):
                pool.dma_start(dst, src).then_inc(stored, 16)
                stores[0] += 1

            gpos = 0
            nv = 0
            for name, rows in VECS:
                v = vec_rows(i_[name])
                r = 0
                while r < rows:
                    k = min(rows - r, 128 - gpos % 128)
                    pool.dma_start(vrows[gpos % 128:gpos % 128 + k, gpos // 128, :], v[r:r + k]).then_inc(vec_in, 16)
                    nv += 1
                    gpos += k
                    r += k
            vec_loads[0] = nv

            def squares(j, n_tiles=8):
                for k in range(n_tiles):
                    c = norm_base[j] + k + 1
                    pool.wait_ge(sq_done, c)
                    if k == 0:
                        if j:
                            pool.wait_ge(ms_done, j)
                        pool.tensor_copy(ssq[:, :], sq[:, (c - 1) % 2, :]).then_inc(ssq_done, 1)
                    else:
                        pool.wait_ge(ssq_done, c - 1)
                        pool.tensor_tensor(ssq[:, :], ssq[:, :], sq[:, (c - 1) % 2, :], ALU.add).then_inc(ssq_done, 1)

            squares(0)

            def rope_cos(q, t_count, table, rows=128):
                table = C(table, rows) if isinstance(table, str) else table
                """qcos = the tile times its cosines, once it is out of PSUM"""
                pool.wait_ge(tile_evac, t_count)
                if q >= 2:
                    pool.wait_ge(rope_done, q - 1)
                pool.tensor_tensor(qcos[0:rows, q % 2, :], qraw[0:rows, q % 2, :], table, ALU.mult).then_inc(cos_done, 1)

            def ffn(layer):
                F0 = NF * layer
                st = V[:, VOFF["state_ffn_conv"] + layer * 88:VOFF["state_ffn_conv"] + layer * 88 + 88].rearrange(
                    "p (r h f) -> p r h f", r=2, h=2)
                pool.wait_ge(stored, 16 * stores[0])
                for j in range(2):
                    ins = pool.memset(upad[:, j, :, 66:68], 0.0)
                ins.then_inc(pads_set, 1)
                pool.wait_ge(rstd_done, norm_of[layer, "ffn"] + 1)

                def step(f, j, first):
                    if not first:
                        pool.wait_ge(ffn_step, (f + (F0 - 2)) * 6 + 4)
                    pool.tensor_copy(upad[:, j, :, 0:2], st[:, :, :, bass.ds(f, 1)].rearrange("p r h f -> p h (r f)")
                                     ).then_inc(hist_done, 1)
                    pool.wait_ge(u_raw, f + (F0 + 1))
                    for c, n_ in ((0, 64), (64, SEQ)):
                        cols_ = slice(c + 2 + 2 * (c > 0), c + 2 + 2 * (c > 0) + n_)
                        ins = pool.tensor_tensor(upad[:, j, :, cols_], upad[:, j, :, cols_],
                                                 rstd[:, c:c + n_].rearrange("p (o n) -> p o n", o=1).to_broadcast([128, 2, n_]), ALU.mult)
                    ins.then_inc(u_evac, 1)
                    pool.wait_ge(u_evac, f + (F0 + 1))
                    for seg, c in ((0, 64), (1, TG)):
                        ins = pool.tensor_copy(
                            ust[:, seg, :, :].rearrange("p r (h f) -> p h r f", h=2)[:, :, :, bass.ds(f, 1)].rearrange("p h r f -> p h (r f)"),
                            upad[:, j, :, c:c + 2])
                    ins.then_inc(ust_done, 1)

                for j in range(2):
                    step(j, j, True)
                with pool.Fori(1, NF // 2) as i:
                    for j in range(2):
                        step(i * 2 + j, j, False)
                squares(norm_next(layer))

            def pool_rwkv(layer):
                s0 = first_slab[layer, "mix"]
                pool.wait_ge(mm_done, done_after[s0 + 11])
                for dst, src in ((L1[:, :, 0:64], i_["b_w1"][0].rearrange("(k p) n -> p k n", p=128)),
                                 (L1[:, :, 64:128], i_["b_a1"][0].rearrange("(k p) n -> p k n", p=128)),
                                 (L1[:, :, 128:256], i_["b_g1"][0].rearrange("(k p) n -> p k n", p=128)),
                                 (L2[0:64, 0, :], i_["b_w2"][0]), (L2[64:128, 0, :], i_["b_a2"][0]), (L2[:, 1, :], i_["b_g2"][0])):
                    pool.dma_start(dst, src).then_inc(lora_in, 16)
                pool.wait_ge(shift_out, 1)
                for z, name in enumerate(("b_shift_sample", "b_shift_prompt")):
                    store(o_[name][0, 0].rearrange("(k q) -> k q", q=128), shot[8 * z:8 * z + 8, :])
                pool.wait_ge(lora_evac, 8)
                flat = LW[:, :, :].rearrange("p k n -> p (k n)")
                pool.tensor_scalar(flat, flat, DECAY, None, ALU.mult).then_inc(lw_done, 1)
                pool.wait_ge(lora_evac, 24)
                for g in range(2):
                    ins = pool.memset(SS[g][:, :, :], 0.0)
                chain(ins)
                for g in range(2):
                    for e in range(2):
                        src = i_["state_b_wkv"][0, 0].rearrange("(g q e) i j -> g e i q j", g=2, e=2)[g, e]
                        pool.dma_start(SS[g][64 * e:64 * e + 64, :, 64 * e:64 * e + 64], src).then_inc(state_in, 16)
                pool.wait_ge(rec_ready, 1)
                for g in range(2):
                    for z in range(4):
                        ins = pool.memset(BD[g][z][:, :, :], 0.0)
                ins.then_inc(built_pool, 1)
                pool.wait_ge(built_pool, 1)
                for c in range(CHUNKS):
                    for g in range(2):
                        if c:
                            taken(pool, g, c - 1, 19)
                            taken(pool, g, c - 1, 20)
                        for z, src in ((0, MX), (3, VV)):
                            for e in range(2):
                                r_ = slice(64 * e, 64 * e + 64)
                                ins = pool.tensor_copy(BD[g][z][r_, :, r_], src[r_, 4 * g:4 * g + 4, 64 * c:64 * c + 64])
                        ins.then_inc(built_pool, 1)
                    if c in (0, CHUNKS - 1):
                        for g in range(2):
                            pool.wait_ge(z_staged, 2 * (c > 0) + g + 1)
                            name = "b_wkv_prompt" if c else "b_wkv_sample"
                            stg = (BD[0][4 + g] if c else SS[g])
                            for e in range(2):
                                dst = o_[name][0, 0].rearrange("(g q e) i j -> g e i q j", g=2, e=2)[g, e]
                                if c:
                                    store(dst, stg[64 * e:64 * e + 64, :, 64 * e:64 * e + 64])
                                else:
                                    pool.dma_start(dst, stg[64 * e:64 * e + 64, :, 64 * e:64 * e + 64]).then_inc(state_stored, 16)
                for k in range(KD):
                    y = R[:, k, :]
                    pool.wait_ge(y_inv, k + 1)
                    chain(pool.tensor_tensor(y, y, MX[:, k, :], ALU.mult))
                    chain(pool.tensor_scalar(y, y, vcol("b_ln_w", k), vcol("b_ln_b", k), ALU.mult, ALU.add))
                    chain(pool.tensor_tensor(y, y, XX[:, k, :], ALU.add))
                    pool.tensor_tensor(y, y, G[:, k, :], ALU.mult).then_inc(y_gated, 1)

            def pool_mla(layer):
                E, Rb, Q = E0[layer], R0[layer], Q0[layer]
                pool.wait_ge(x_done, 8 * xs_of[norm_of[layer, "mix"]] + 8)
                chain(pool.memset(cr[:, :], 0.0))
                pool.dma_start(cl[:, :], i_["cache_c_latent"][0, 0]).then_inc(cache_in, 16)
                pool.dma_start(cr[:, 64:96], i_["cache_c_rope"][0, 0]).then_inc(cache_in, 16)
                squares(norm_of[layer, "cq"], 4)
                squares(norm_of[layer, "ckv"], 2)
                pool.wait_ge(placed, 1)
                rope_cos(Rb, E + 7, "cos_c", 96)
                pool.wait_ge(rope_done, Rb + 1)
                kpe = KPE[64:96, :].rearrange("p (o n) -> p o n", o=1).to_broadcast([32, 16, T])
                pool.tensor_copy(KC[64:96, :, PAST:KEYS], kpe).then_inc(kc_rope, 1)
                pool.wait_ge(kc_rope, 1)
                for z, (c, n_) in enumerate(TILES):
                    pool.wait_ge(rows_out, ROWS_BEFORE[layer] + z + 1)
                    for name, src in (("c_lat", lato[0:n_, z, :]), ("c_rope", ropeo[0:n_, z, 64:96])):
                        store(o_[name + "_sample"][0, 0] if z == 0 else o_[name + "_prompt"][0, 0, 128 * (z - 1):128 * z], src)
                for h in range(4):
                    rope_cos(Rb + 1 + h, E + 31 + h + 1, "cos_c", 96)
                for p in range(PAIRS):
                    if p + 2 < PAIRS:
                        rope_cos(Rb + 5 + 2 * p, E + 35 + 2 * p + 1, "cos_c", 96)
                    if p + 2 < PAIRS:
                        rope_cos(Rb + 6 + 2 * p, E + 36 + 2 * p + 1, "cos_c", 96)

            for layer in range(DEPTH):
                mixer, inst = layer % 3, layer // 3
                if mixer == 0:
                    if inst:
                        pool.wait_ge(x_done, 8 * xs_of[norm_of[layer, "mix"]] + 8)
                    for dup in range(2):
                        for g in range(2):
                            pool.dma_start(ck[:, g, dup, :], i_["cache_a_k"][inst, 0, :, g, :]).then_inc(cache_in, 16)
                        pool.dma_start(ci[:, dup, :], i_["cache_a_idx"][inst, 0]).then_inc(cache_in, 16)
                    pool.dma_start(Vc[:, :], i_["cache_a_v"][inst, 0].rearrange("p g d -> p (g d)")).then_inc(cache_in, 16)
                    pool.wait_ge(rstd_done, norm_of[layer, "mix"] + 1)
                    pool.tensor_tensor(cosr[:, :], C("cos_a"), rstd[:, :], ALU.mult).then_inc(cosr_done, 1)
                    pool.wait_ge(cosr_done, inst + 1)
                    for r_, t_ in enumerate(A_ROPE[:9 - 2]):
                        rope_cos(R0[layer] + r_, E0[layer] + t_ + 1, cosr[:, :])
                    for z, (c, n_) in enumerate(TILES):
                        pool.wait_ge(rows_out, ROWS_BEFORE[layer] + z + 1)
                        if z == 0:
                            dst = [o_[q][inst, 0] for q in ("a_k_sample", "a_v_sample", "a_idx_sample")]
                        else:
                            dst = [o_[q][inst, 0, 128 * (z - 1):128 * z] for q in ("a_k_prompt", "a_v_prompt", "a_idx_prompt")]
                        store(dst[0].rearrange("p g d -> p (g d)"), Ko[0:n_, z, :])
                        store(dst[1].rearrange("p g d -> p (g d)"), Vt[0:n_, z, :])
                        store(dst[2], KIo[0:n_, z, :])
                    for p in range(EARLY):
                        rope_cos(R0[layer] + 7 + p, E0[layer] + 9 + p + 1, cosr[:, :])
                    pool.wait_ge(mask_done, inst + 1)
                    pool.dma_start(MK[64:128, 384:576], MK[0:64, 384:576]).then_inc(mask_copied, 16)
                    for p in range(EARLY, PAIRS):
                        rope_cos(R0[layer] + 7 + p, E0[layer] + 9 + p + 1, cosr[:, :])
                    squares(norm_of[layer, "ffn"])
                elif mixer == 1:
                    pool_rwkv(layer)
                    squares(norm_of[layer, "ffn"])
                else:
                    pool_mla(layer)
                    squares(norm_of[layer, "ffn"])
                ffn(layer)
                pool.wait_ge(ust_copied, layer + 1)
                for z, name in enumerate(("ffn_sample", "ffn_prompt")):
                    store(o_[name][layer, 0].rearrange("r (c q) -> (r c) q", q=128), uout[0:88, z, :])
                STORES_AT[layer + 1] = stores[0]
            for z, (c, n_) in enumerate(TILES):
                pool.wait_ge(y_copied, KD)
                store(o_["y_sample"][0] if z == 0 else o_["y_prompt"][0, 128 * (z - 1):128 * z], xin[0:n_, z, :])
            pool.wait_ge(stored, 16 * stores[0])
            pool.wait_ge(state_stored, 64)

        @block.tensor
        def _(pe):
            ident, ones = C("ident"), C("ones")

            def ready(n):
                pe.wait_ge(w_lo, n + 1)

            def parts(n):
                s = slabs[n]
                return (t[n % 2][:, 0:s.kt * s.w].rearrange("p (k w) -> p k w", w=s.w) for t in (hi, lo))

            def product(out, n, c0, xh, xl, m=128, start=True, stop=True, before=None):
                wh, wl = parts(n)
                kt = slabs[n].kt
                for k in range(kt):
                    if before:
                        before(k)
                    a, b = wh[:, k, c0:c0 + m], wl[:, k, c0:c0 + m]
                    pe.matmul(out, a, xh(k), start=(start and k == 0), stop=False)
                    pe.matmul(out, a, xl(k), start=False, stop=False)
                    last = pe.matmul(out, b, xh(k), start=False, stop=(stop and k == kt - 1))
                last.then_inc(mm_done, 1)

            def x_ready(j):
                return lambda k: pe.wait_ge(xn_done, XN[j] + k + 1)

            def turn(out, in_):
                n_ = in_.shape[0]
                return pe.transpose(out, in_, ident[0:n_, 0:n_])

            def mean_square(j):
                pe.wait_ge(ssq_done, norm_base[j + 1])
                pe.matmul(psum[7][:, 0:T], ones, ssq[:, :], start=True, stop=True).then_inc(ms_done, 1)

            pe.wait_ge(con_in, 16)
            pe.wait_ge(vec_in, 16 * vec_loads[0])
            for g in range(VGROUPS):
                n_ = min(128, NVEC - 128 * g)
                if g >= 2:
                    pe.wait_ge(v_copied, g - 1)
                turn(psum[2 + g % 2][:, 0:n_], vrows[0:n_, g, :]).then_inc(vt_ready, 1)
            pe.wait_ge(x_in, 48)
            for k in range(KD):
                if k >= 2:
                    pe.wait_ge(x_done, k - 1)
                for z, (c, n_) in enumerate(TILES):
                    last = turn(psum[k % 2][:, c:c + n_], xin[0:n_, z, k * 128:(k + 1) * 128])
                last.then_inc(xt_ready, 1)
            def qk(q, qt, kt_of, kdim):
                if q:
                    pe.wait_ge(max_done, q)
                for e in range(2):
                    Q_, K_ = qt(e), kt_of(e)
                    pe.matmul(psum[3 + e][:, 0:128], Q_[:, 64:192], K_[:, 192:320], start=True, stop=True)
                    pe.matmul(psum[3 + e][:, 128:384], Q_[:, 192:320], K_[:, 192:448], start=True, stop=True)
                    last = pe.matmul(psum[5][64 * e:64 * e + 64, 0:192], Q_[:, 0:64], K_[:, 0:192], start=True, stop=True)
                last.then_inc(qk_done, 1)

            def turn_probs(q):
                pe.wait_ge(prob_done, q + 1)
                if q:
                    pe.wait_ge(pt_act, q)
                    pe.wait_ge(pt_dve, q)
                L = LS(q)
                for e in range(2):
                    b, o = psum[6 + e], 384 * e
                    turn(b[:, 0:128], L[:, o:o + 128])
                    turn(b[:, 128:256], L[:, o + 128:o + 256])
                    turn(b[:, 256:384], L[:, o + 256:o + 384])
                turn(psum[6][:, 384:512], L[:, 768:896])
                turn(psum[7][0:64, 384:512], L[:, 896:960]).then_inc(pt_turned, 1)

            def values(q, vals):
                pe.wait_ge(pt_act, q + 1)
                pe.wait_ge(pt_dve, q + 1)
                if q:
                    pe.wait_ge(ol_done, q)
                for e in range(2):
                    vc, vs, v0, v1 = vals(e)
                    out = psum[2][64 * e:64 * e + 64, :]
                    o = 512 * e
                    pe.matmul(out[:, 64:320], v0, PT[:, o:o + 256], start=True, stop=False, skip_group_check=True)
                    pe.matmul(out[:, 192:320], v1, PT[:, o + 256:o + 384], start=False, stop=True, skip_group_check=True)
                    pe.matmul(out[:, 0:64], vc, PT[:, 384 + 64 * e:448 + 64 * e], start=True, stop=False, skip_group_check=True)
                    last = pe.matmul(out[:, 0:64], vs, PT[0:64, 896 + 64 * e:960 + 64 * e], start=False, stop=True,
                                     skip_group_check=True)
                last.then_inc(pv_done, 1)

            def mixer_out(layer, xh, xl, wait):
                s0 = first_slab[layer, "out"]
                xb = 8 * xs_of[norm_of[layer, "ffn"]]
                wait()
                for m in range(KD):
                    n = s0 + m // 2
                    if m % 2 == 0:
                        ready(n)
                    if m >= 2:
                        pe.wait_ge(x_done, xb + m - 1)
                    product(psum[4 + m % 2][:, 0:T], n, 128 * (m % 2), xh, xl)

            def ffn(layer):
                F0 = NF * layer
                u0, d0 = first_slab[layer, "up"], first_slab[layer, "down"]
                jn = norm_of[layer, "ffn"]

                def up(f, n, j, first, before=None):
                    pe.wait_ge(w_lo, f + (u0 + 1))
                    if not first:
                        pe.wait_ge(u_raw, f + (F0 - 1))
                    for h in range(2):
                        product(psum[2 * j + h][:, 0:T], n, 128 * h, lambda k: XH[:, k, :], lambda k: XL[:, k, :],
                                before=before if h == 0 else None)
                        if before and h == 0:
                            mean_square(jn)

                for j in range(2):
                    up(j, u0 + j, j, True, x_ready(jn) if j == 0 else None)
                with pe.Fori(1, NF // 2) as i:
                    for j in range(2):
                        up(i * 2 + j, u0 + j, j, False)

                xb = 8 * xs_of[norm_next(layer)]

                def down(m, j, first):
                    for half in range(2):
                        pe.wait_ge(w_lo, m * 2 + (d0 + half + 1))
                        if half == 0 and not first:
                            pe.wait_ge(x_done, m + (xb - 1))
                        if first:
                            pe.wait_ge(g_done, F0 + 11 * (half + 1))
                        product(psum[4 + j][:, 0:TG], d0 + 2 * j + half, 0, lambda k: GH[:, 11 * half + k, :],
                                lambda k: GL[:, 11 * half + k, :], start=(half == 0), stop=(half == 1))

                down(0, 0, True)
                pe.wait_ge(ust_done, F0 + NF)
                for z in range(2):
                    last = turn(psum[6][0:88, 128 * z:128 * z + 128], ust[:, z, :, :].rearrange("p r c -> p (r c)"))
                last.then_inc(ust_turned, 1)
                down(1, 1, True)
                with pe.Fori(1, KD // 2) as i:
                    for j in range(2):
                        down(i * 2 + j, j, False)
                if norm_next(layer) not in LATE:
                    mean_square(norm_next(layer))

            def dsa(layer):
                inst, s0, jn = layer // 3, first_slab[layer, "mix"], norm_of[layer, "mix"]
                E, Rb, Q = E0[layer], R0[layer], Q0[layer]
                slab_of = [0, 0, 0, 1, 1, 2, 2, 3, 3] + [4 + j // 2 for j in range(8)]
                col_of = [0, 128, 136, 0, 128, 0, 128, 0, 128] + [128 * (j % 2) for j in range(8)]

                def project(t):
                    n = s0 + slab_of[t]
                    ready(n)
                    if t >= 2:
                        pe.wait_ge(tile_evac, E + t - 1 + (t >= 9))
                    product(psum[0 if t >= 9 or t % 2 == 0 else 2][:, 0:T], n, col_of[t], lambda k: XH[:, k, :],
                            lambda k: XL[:, k, :], before=x_ready(jn) if t == 0 else None)
                    if t == 0:
                        mean_square(jn)

                def perm(r):
                    pe.wait_ge(tile_evac, E + A_ROPE[r] + 1)
                    if r:
                        pe.wait_ge(rope_done, Rb + r)
                    pe.matmul(psum[1][:, 0:T], C("perm_a"), qraw[:, (Rb + r) % 2, :], start=True, stop=True).then_inc(perm_done, 1)

                r = 0
                for t in range(9):
                    project(t)
                    if t >= 1 and t - 1 in A_ROPE:
                        perm(r)
                        r += 1
                perm(r)
                pe.wait_ge(cache_in, 16 * CACHE_LOADS[layer])
                for g in range(2):
                    turn(psum[3][:, 128 * g:128 * g + 128], ck[:, g, :, :].rearrange("p u d -> p (u d)"))
                turn(psum[3][:, 256:384], ci[:, :, :].rearrange("p u d -> p (u d)")).then_inc(turned, 1)
                pe.wait_ge(rope_done, Rb + 3)
                pe.wait_ge(rows_scaled, inst + 1)
                for z, (c, n_) in enumerate(TILES):
                    b = psum[(6, 7, 4)[z]]
                    for g in range(2):
                        turn(b[0:n_, 64 * g:64 * g + 64], KT[0:64, g, PAST + c:PAST + c + n_])
                    turn(b[0:n_, 128:256], VTf[:, c:c + n_])
                    turn(b[0:n_, 256:320], KIT[0:64, PAST + c:PAST + c + n_])
                    turn(b[0:n_, 320:448], WIf[:, c:c + n_]).then_inc(rows_turned, 1)
                pe.wait_ge(rope_done, Rb + 7)
                pe.wait_ge(turned_in, inst + 1)
                pe.wait_ge(rows_out, ROWS_BEFORE[layer] + 3)
                for h in range(8):
                    if h >= 2:
                        pe.wait_ge(relu_done, 8 * inst + h - 1)
                    r_ = slice(64 * (h % 2), 64 * (h % 2) + 64)
                    q_, k_ = QIT[r_, h // 2, :], KIT[r_, :]
                    main, samp = psum[3 + h % 2], psum[5 + h % 2]
                    pe.matmul(main[:, 0:128], q_[:, 64:192], k_[:, 192:320], start=True, stop=True)
                    pe.matmul(main[:, 128:384], q_[:, 192:320], k_[:, 192:448], start=True, stop=True)
                    pe.matmul(samp[0:64, 0:192], q_[:, 0:64], k_[:, 0:192], start=True, stop=True).then_inc(dots_done, 1)
                for p in range(EARLY):
                    project(9 + p)
                    perm(7 + p)

                def pair_qk(p):
                    pe.wait_ge(rope_done, Rb + 8 + p)
                    if p == 0:
                        pe.wait_ge(relu_done, 8 * inst + 8)
                    qk(Q + p, lambda e: QD[64 * e:64 * e + 64, p, :], lambda e: KT[64 * e:64 * e + 64, p // 4, :], 64)

                pair_qk(0)
                pair_qk(1)
                for p in range(PAIRS):
                    if p + EARLY < PAIRS:
                        project(9 + EARLY + p)
                    turn_probs(Q + p)
                    if p + 2 < PAIRS:
                        pair_qk(p + 2)
                    if p + EARLY < PAIRS:
                        perm(7 + EARLY + p)
                    g = slice(64 * (p // 4), 64 * (p // 4) + 64)
                    values(Q + p, lambda e: (Vc[:, g], Vt[0:64, 0, g], Vt[:, 1, g], Vt[:, 2, g]))
                mixer_out(layer, lambda k: OH[:, k, :], lambda k: OL[:, k, :], lambda: pe.wait_ge(ol_done, Q + PAIRS))

            def pe_rwkv(layer):
                s0 = first_slab[layer, "mix"]
                pe.wait_ge(shift_set, 1)
                pe.transpose(psum[6][0:16, 0:128], sho[:, :], ident).then_inc(shift_turned, 1)
                for i in range(24):
                    n = s0 + i // 2
                    ready(n)
                    pe.wait_ge(mix_done, i // 8 + 1)
                    if i >= 4:
                        pe.wait_ge(rkv_evac, i - 3)
                    product(psum[i % 4][:, 0:T], n, 128 * (i % 2), lambda k: XH[:, k, :], lambda k: XL[:, k, :])
                pe.wait_ge(lora_in, 96)
                pe.wait_ge(rkv_evac, 24)
                for a in range(3):
                    r_ = (slice(0, 64), slice(64, 128), slice(0, 128))[a]
                    c_ = (slice(0, 64), slice(64, 128), slice(128, 256))[a]
                    pe.wait_ge(mix_done, 4 + a)
                    for k in range(KD):
                        last = pe.matmul(psum[4 + a][r_, 0:T], L1[:, k, c_], MX[:, k, :], start=(k == 0), stop=(k == KD - 1))
                    last.then_inc(lora_mid, 1)
                    pe.wait_ge(lora_act, a + 1)
                    for m in range(KD):
                        i = 8 * a + m
                        if i >= 4:
                            pe.wait_ge(lora_evac, i - 3)
                        pe.matmul(psum[i % 4][:, 0:T], L2[r_, int(a == 2), 128 * m:128 * m + 128], (LTg if a == 2 else LT)[r_, :],
                                  start=True, stop=True).then_inc(lora_out, 1)

                def head_sums(src, base_, wait, free):
                    for k in range(KD):
                        wait(k)
                        free(k)
                        pe.matmul(psum[k % 4][:, 0:T], C("headsum"), src[:, k, :], start=True, stop=True).then_inc(hs_done, 1)

                pe.wait_ge(lora_evac, 24)
                head_sums(XX, 0, lambda k: pe.wait_ge(kk_sq, 1), lambda k: k < 4 or pe.wait_ge(hs_root, k - 3))
                pe.wait_ge(hs_root, 8)
                head_sums(XX, 8, lambda k: pe.wait_ge(bonus_in, k + 1), lambda k: k < 4 or pe.wait_ge(bonus_out, k - 3))
                pe.wait_ge(state_in, 64)
                pe.wait_ge(rec_ready, 1)
                for g in range(2):
                    for q in range(4):
                        last = turn(psum[4 * g][:, 128 * q:128 * q + 128], SS[g][:, q, :])
                    last.then_inc(state_turned, 1)

                def recurrence(c):
                    cols_ = slice(64 * c, 64 * c + 64)
                    for z, (name, _, needs) in enumerate(STAGES):
                        for g in range(2):
                            b = BD[g]
                            vt, bt, kt, Z = BX[g]
                            bank = psum[4 * g + z % 4]
                            if z == 0:
                                pe.wait_ge(built_pool, 2 * c + g + 2)
                                pe.wait_ge(built_dve, 2 * c + g + 1)
                                if c == 0:
                                    pe.wait_ge(state_set, g + 1)
                                if c == 1:
                                    pe.wait_ge(z_staged, g + 1)
                            if z < 4 and c:
                                taken(pe, g, c - 1, 20 + z)
                            if name == "rhs":
                                pe.wait_ge(state_set, 2 * (c > 0) + g + 1)
                                if c:
                                    taken(pe, g, c - 1, 23)
                            for q_ in needs:
                                taken(pe, g, c, q_)

                            def mm(lhs, rhs, n_=128, start=True, stop=True, o=0):
                                for q in range(4):
                                    r = rhs(q) if callable(rhs) else rhs[:, q, :]
                                    x = pe.matmul(bank[:, o + n_ * q:o + n_ * q + n_], lhs[:, q, :], r, start=start, stop=stop,
                                                  skip_group_check=True)
                                return x

                            if name == "arT":
                                mm(b[1], lambda q: R[:, 4 * g + q, cols_], 64)
                                last = mm(b[2], lambda q: R[:, 4 * g + q, cols_], 64, o=256)
                            elif name in ("vt", "bt", "kt"):
                                src = b[{"vt": 3, "bt": 1, "kt": 2}[name]]
                                for q in range(4):
                                    last = turn(bank[:, 128 * q:128 * q + 128], src[:, q, :])
                            elif name in ("rhs", "z", "y"):
                                for q in range(4):
                                    if name == "rhs":
                                        terms = ((b[0][:, q, :], Z[:, q, :]), (b[7][:, q, :], vt[:, q, :]))
                                    elif name == "z":
                                        terms = ((bt[:, q, :], b[1][:, q, :]), (kt[:, q, :], vt[:, q, :]))
                                    else:
                                        ar = b[8][:, :, :].rearrange("p a (b n) -> p (a b) n", n=64)
                                        terms = ((Z[:, q, :], R[:, 4 * g + q, cols_]), (b[1][:, q, :], ar[:, q, :]),
                                                 (vt[:, q, :], ar[:, 4 + q, :]))
                                    n_ = 64 if name == "y" else 128
                                    for w, (l_, r_) in enumerate(terms):
                                        last = pe.matmul(bank[:, n_ * q:n_ * q + n_], l_, r_, start=(w == 0),
                                                         stop=(w == len(terms) - 1), skip_group_check=True)
                            else:
                                l_, r_ = {"mT": (1, 0), "m": (0, 1), "nT": (2, 0), "m2": (4, 5), "m2T": (5, 4), "p2": (1, 9),
                                          "m4": (2, 1), "m4T": (1, 2), "p4": (5, 3), "m8": (4, 5), "p8": (1, 9), "qT": (6, 3),
                                          "q": (3, 6), "q2": (4, 5), "h": (1, 2), "x1": (3, 4), "u": (9, 5)}[name]
                                last = mm(b[l_], b[r_])
                            last.then_inc(stage_pe[g], 1)

                for c in range(CHUNKS):
                    recurrence(c)
                    if c in (0, CHUNKS - 1):
                        for g in range(2):
                            taken(pe, g, c, 23)
                            taken(pe, g, c, 20)
                            for q in range(4):
                                last = turn(psum[4 * g][:, 128 * q:128 * q + 128], BX[g][3][:, q, :])
                            last.then_inc(z_turned, 1)
                for g in range(2):
                    for z in (20, 21, 22, 23):
                        taken(pe, g, CHUNKS - 1, z)
                pe.wait_ge(z_staged, 4)
                head_sums(R, 16, lambda k: None, lambda k: k < 4 or pe.wait_ge(y_mean, k - 3))
                pe.wait_ge(y_mean, 8)
                head_sums(MX, 24, lambda k: pe.wait_ge(y_sq, k + 1), lambda k: k < 4 or pe.wait_ge(y_root, k - 3))
                pe.wait_ge(y_root, 8)
                mixer_out(layer, lambda k: XH[:, k, :], lambda k: XL[:, k, :], lambda: pe.wait_ge(y_parts, 8))

            def pe_mla(layer):
                s0, jn = first_slab[layer, "mix"], norm_of[layer, "mix"]
                E, Rb, Q = E0[layer], R0[layer], Q0[layer]
                for t in range(7):
                    n = s0 + min(t // 2, 2)
                    ready(n)
                    if t >= 2:
                        pe.wait_ge(tile_evac, E + t - 1)
                    product(psum[0 if t % 2 == 0 else 2][:, 0:T], n, 160 if t == 6 else 128 * (t % 2), lambda k: XH[:, k, :],
                            lambda k: XL[:, k, :], before=x_ready(jn) if t == 0 else None)
                    if t == 0:
                        mean_square(jn)
                pe.wait_ge(tile_evac, E + 7)
                kpe = qraw[:, Rb % 2, :]
                pe.matmul(psum[3][0:96, 0:T], C("place"), kpe, start=True, stop=True)
                pe.matmul(psum[1][0:96, 0:T], C("place_rot"), kpe, start=True, stop=True).then_inc(perm_done, 1)
                pe.wait_ge(cache_in, 16 * CACHE_LOADS[layer])
                for k in range(2):
                    turn(psum[6][:, 128 * k:128 * k + 128], cl[:, 128 * k:128 * k + 128])
                turn(psum[6][0:96, 256:384], cr[:, :]).then_inc(mla_turned, 1)
                mean_square(norm_of[layer, "cq"])
                pe.wait_ge(rms_done, norm_of[layer, "cq"] + 1)
                mean_square(norm_of[layer, "ckv"])
                pe.wait_ge(latf_done, 2)
                pe.wait_ge(rope_done, Rb + 1)
                pe.wait_ge(rms_done, norm_of[layer, "ckv"] + 1)
                pe.wait_ge(mla_cached, 1)
                for z, (c, n_) in enumerate(TILES):
                    b = psum[(7, 6, 4)[z]]
                    for k in range(2):
                        turn(b[0:n_, 128 * k:128 * k + 128], LATF[:, k, PAST + c:PAST + c + n_])
                    turn(b[0:n_, 256:352], KPE[:, c:c + n_]).then_inc(rows_turned, 1)
                pe.wait_ge(lat_parts, 1)
                for j in range(2):
                    n = s0 + 3 + j
                    ready(n)
                    wh, wl = parts(n)
                    for st, c in enumerate((0, 128, 192, 320)):
                        e_ = 7 + 12 * j + st
                        pe.wait_ge(tile_evac, E + e_ - 1)
                        b = psum[0 if e_ % 2 == 0 else 2]
                        for k in range(2):
                            vh, vl = (w[:, k, :].rearrange("p (h c) -> p h c", c=128)[:, :, 64:128] for w in (wh, wl))
                            pe.matmul(b[:, 0:512], LATH[:, k, c:c + 128], vh, start=(k == 0), stop=False)
                            pe.matmul(b[:, 0:512], LATH[:, k, c:c + 128], vl, start=False, stop=False)
                            last = pe.matmul(b[:, 0:512], LATL[:, k, c:c + 128], vh, start=False, stop=(k == 1))
                        last.then_inc(mm_done, 1)
                    for h in range(8):
                        e_ = 11 + 12 * j + h
                        pe.wait_ge(tile_evac, E + e_ - 1)
                        product(psum[0 if e_ % 2 == 0 else 2][:, 0:KEYS], n, 128 * h, lambda k: LATH[:, k, :], lambda k: LATL[:, k, :])

                def project(h):
                    n = s0 + 5 + h // 4
                    ready(n)
                    pe.wait_ge(tile_evac, E + 31 + h)
                    if h == 0:
                        pe.wait_ge(cqn_done, 4)
                    product(psum[0][0:96, 0:T], n, 96 * (h % 4), lambda k: XH[:, k, :], lambda k: XL[:, k, :], m=96)

                def perm(h):
                    pe.wait_ge(tile_evac, E + 31 + h + 1)
                    pe.wait_ge(rope_done, Rb + 1 + h)
                    pe.matmul(psum[1][0:96, 0:T], C("perm_c", 96), qraw[0:96, (Rb + 1 + h) % 2, :], start=True, stop=True
                              ).then_inc(perm_done, 1)

                for h in range(4):
                    project(h)
                    perm(h)

                def pair_qk(p):
                    pe.wait_ge(rope_done, Rb + 1 + 2 * p + 2)
                    if p == 0:
                        pe.wait_ge(kc_rope, 1)
                        pe.wait_ge(mla_cached, 1)
                        pe.wait_ge(rows_out, ROWS_BEFORE[layer] + 3)
                        pe.wait_ge(placed, 1)
                    qk(Q + p, lambda e: QT[0:96, p % 2, e, :], lambda e: KC[0:96, 2 * p + e, :], 96)

                pair_qk(0)
                for p in range(PAIRS):
                    if p + 2 < PAIRS:
                        project(2 * p + 4)
                    turn_probs(Q + p)
                    if p + 1 < PAIRS:
                        pair_qk(p + 1)
                    if p + 2 < PAIRS:
                        perm(2 * p + 4)
                        project(2 * p + 5)

                    def vals(e):
                        c = slice(64 * (2 * p + e), 64 * (2 * p + e) + 64)
                        return VC[:, 0, c], VC[0:64, 1, c], VC[:, 2, c], VC[:, 3, c]
                    values(Q + p, vals)
                    if p + 2 < PAIRS:
                        perm(2 * p + 5)
                mixer_out(layer, lambda k: OH[:, k, :], lambda k: OL[:, k, :], lambda: pe.wait_ge(ol_done, Q + PAIRS))

            for layer in range(DEPTH):
                (dsa, pe_rwkv, pe_mla)[layer % 3](layer)
                ffn(layer)
            for k in range(KD):
                pe.wait_ge(xn_done, XN[norm_final] + k + 1)
                if k >= 2:
                    pe.wait_ge(y_copied, k - 1)
                for z, (c, n_) in enumerate(TILES):
                    last = turn(psum[k % 2][0:n_, 128 * z:128 * z + 128], xn[:, k % 2, c:c + n_])
                last.then_inc(y_turned, 1)

        @block.scalar
        def _(act):
            chain = Chain(act, act_c)

            def split_hi(n, n_expr=None, raw_count=None):
                s_ = slabs[n]
                act.wait_ge(w_raw[n % 2], raw_after[n] if raw_count is None else raw_count)
                if n_expr is None:
                    if n >= 2:
                        act.wait_ge(mm_done, done_after[n - 2])
                else:
                    act.wait_ge(mm_done, n_expr)
                w_ = s_.kt * s_.w
                act.activation(hi[n % 2][:, 0:w_], raw[n % 2][:, 0:w_], ACT.Copy).then_inc(w_hi, 1)

            def squares(j, src, count):
                for k in range(NORMS[j][1]):
                    square(j, k, src(k), count(k))

            def square(j, k, src, wait):
                wait()
                c = norm_base[j] + k + 1
                if c > 2:
                    act.wait_ge(ssq_done, c - 2)
                act.activation(sq[:, (c - 1) % 2, :], src, ACT.Square).then_inc(sq_done, 1)

            def root(j):
                act.wait_ge(ms_done, j + 1)
                n_ = 128.0 * NORMS[j][1]
                act.activation(rms[:, :], psum[7][:, 0:T], ACT.Sqrt, bias=eps_col, scale=1.0 / n_).then_inc(rms_done, 1)

            eps_col = C("eps")[:, 0:1]
            act.wait_ge(con_in, 16)
            for g in range(VGROUPS):
                n_ = min(128, NVEC - 128 * g)
                act.wait_ge(vt_ready, g + 1)
                act.copy(V[:, 128 * g:128 * g + n_], psum[2 + g % 2][:, 0:n_]).then_inc(v_copied, 1)
            for k in range(KD):
                square(0, k, xT[:, k, :], lambda: act.wait_ge(x_done, k + 1))
            split_hi(0)

            def exps(q):
                act.wait_ge(max_done, q + 1)
                for u, (a, b) in enumerate(UNITS):
                    ins = act.activation(LS(q)[:, a:b], LS(q)[:, a:b], ACT.Exp, scale=-1.0,
                                         bias=negmax[:, slot(q), u:u + 1], accum_out=sums[:, slot(q), u:u + 1])
                ins.then_inc(exp_done, 1)

            def pt_copy(q):
                act.wait_ge(pt_turned, q + 1)
                if q:
                    act.wait_ge(pv_done, q)
                act.copy(PT[:, 512:896], psum[7][:, 0:384])
                act.copy(PT[0:64, 896:1024], psum[7][0:64, 384:512]).then_inc(pt_act, 1)

            def out_hi(q, p):
                act.wait_ge(pv_done, q + 1)
                act.copy(OH[:, p, :], psum[2][:, 0:T]).then_inc(oh_done, 1)

            def mixer_out(layer):
                s0, j = first_slab[layer, "out"], norm_of[layer, "ffn"]
                xb = 8 * xs_of[j]
                for m in range(KD):
                    if m % 2 == 0:
                        split_hi(s0 + m // 2 + 1)
                    square(j, m, xT[:, m, :], lambda: act.wait_ge(x_done, xb + m + 1))

            def ffn(layer):
                F0 = NF * layer
                u0, d0 = first_slab[layer, "up"], first_slab[layer, "down"]
                jn = norm_next(layer)
                act.wait_ge(pads_set, layer + 1)

                def activate(f):
                    act.wait_ge(ffn_step, (f + (F0 - 1)) * 6 + 4)
                    act.activation(silu[:, :], conv[:, f_par[0], 0, :], ACT.Silu).then_inc(silu_done, 1)

                f_par = [0]

                split_hi(u0 + 1)
                root(norm_of[layer, "ffn"])

                def step(f, j, n_later, raw_count, mm_free, first, tile0):
                    act.wait_ge(mm_done, f * 2 + (done_after[u0] - 2 + 2))
                    if not tile0:
                        act.wait_ge(ust_done, f + (F0 - 1))
                    ps = [psum[2 * j], psum[2 * j + 1]]
                    for h in range(2):
                        act.copy(upad[:, j, h, 2:66], ps[h][:, 0:64])
                        ins = act.copy(upad[:, j, h, 68:TG + 2], ps[h][:, 64:T])
                    ins.then_inc(u_raw, 1)
                    split_hi(n_later, mm_free, raw_count)
                    if not first:
                        f_par[0] = 1 - j
                        activate(f)
                    act.wait_ge(u_evac, f + (F0 + 1))
                    w_ = VOFF["f_w_conv"] + (layer * 3 + 2) * 44
                    b_ = VOFF["f_b_conv"] + layer * 44
                    for h in range(2):
                        ins = act.activation(conv[:, j, h, :], upad[:, j, h, 2:TG + 2], ACT.Identity,
                                             scale=V[:, bass.ds(f + (w_ + NF * h), 1)], bias=V[:, bass.ds(f + (b_ + NF * h), 1)])
                    ins.then_inc(c2_done, 1)

                for j in range(2):
                    n = u0 + j
                    step(j, j, n + 2, raw_after[n + 2], done_after[n], j == 0, True)
                with act.Fori(1, NF // 2 - 1) as i:
                    for j in range(2):
                        n = u0 + 2 + j
                        step(i * 2 + j, j, n + 2, (i - 1) * 32 + raw_after[n + 2], (i - 1) * 4 + done_after[n], False, False)
                for j in range(2):
                    n = u0 + NF - 2 + j
                    step(NF - 2 + j, j, n + 2, raw_after[n + 2], done_after[n], False, False)
                f_par[0] = 1
                activate(NF)

                xb = 8 * xs_of[jn]

                def down(m, k, raw2, mm2, sq_wait):
                    for half in range(2):
                        n = d0 + 2 * k + half + 1
                        if n > d0 + 1 and n < N:
                            split_hi(n, mm2 and mm2(half), raw2 and raw2(half))
                    c = m + norm_base[jn]
                    act.wait_ge(x_done, m + (xb + 1))
                    act.wait_ge(ssq_done, c - 1)
                    act.activation(sq[:, (norm_base[jn] + k) % 2, :], xT[:, bass.ds(m, 1), :].rearrange("p o n -> p (o n)"), ACT.Square).then_inc(sq_done, 1)

                down(0, 0, None, None, None)
                act.wait_ge(ust_turned, layer + 1)
                if layer:
                    act.wait_ge(stored, 16 * STORES_AT[layer])
                act.copy(uout[0:88, :, :], psum[6][0:88, 0:256].rearrange("p (z q) -> p z q", z=2)).then_inc(ust_copied, 1)
                down(1, 1, None, None, None)
                with act.Fori(1, KD // 2 - 1) as i:
                    for j in range(2):
                        down(i * 2 + j, 2 + j,
                             lambda half: (i - 1) * 32 + raw_after[d0 + 2 * (2 + j) + half + 1],
                             lambda half: (i - 1) * 4 + done_after[d0 + 2 * (2 + j) + half - 1], None)
                for m in (KD - 2, KD - 1):
                    down(m, m, None, None, None)
                if jn not in LATE:
                    root(jn)

            def dsa(layer):
                inst, s0 = layer // 3, first_slab[layer, "mix"]
                E, Rb, Q = E0[layer], R0[layer], Q0[layer]
                firsts = {0: 0, 3: 1, 5: 2, 7: 3, 9: 4, 11: 5, 13: 6, 15: 7}
                done = done_after[s0 - 1] if s0 else 0

                def evac(t):
                    if t in firsts:
                        split_hi(s0 + firsts[t] + 1)
                    if t == 0:
                        root(norm_of[layer, "mix"])
                    act.wait_ge(mm_done, done + t + 1)
                    if t == 2:
                        dst = WIf[:, :]
                    elif t == 4:
                        dst = VTf[:, :]
                    else:
                        r = Rb + A_ROPE.index(t)
                        if r >= 2:
                            act.wait_ge(perm_done, r - 1)
                            act.wait_ge(cos_done, r - 1)
                        dst = qraw[:, r % 2, :]
                    act.copy(dst, psum[0 if t >= 9 or t % 2 == 0 else 2][:, 0:T]).then_inc(tile_evac, 1)

                for t in range(9):
                    evac(t)
                for z, (c, n_) in enumerate(TILES):
                    act.wait_ge(rows_turned, ROWS_BEFORE[layer] + z + 1)
                    b = psum[(6, 7, 4)[z]]
                    act.copy(Ko[0:n_, z, :], b[0:n_, 0:128])
                    act.copy(Vt[0:n_, z, :], b[0:n_, 128:256])
                    act.copy(KIo[0:n_, z, :], b[0:n_, 256:320])
                    act.copy(WI[0:n_, z, :], b[0:n_, 440:448]).then_inc(rows_out, 1)
                for h in range(8):
                    act.wait_ge(dots_done, 8 * inst + h + 1)
                    if h >= 2:
                        act.wait_ge(score_done, 8 * inst + h - 1)
                    act.activation(relu[:, h % 2, 0:384], psum[3 + h % 2][:, 0:384], ACT.Relu)
                    act.activation(relu[0:64, h % 2, 384:576], psum[5 + h % 2][0:64, 0:192], ACT.Relu).then_inc(relu_done, 1)
                for p in range(EARLY):
                    evac(9 + p)
                exps(Q)
                exps(Q + 1)
                for p in range(PAIRS):
                    if p + EARLY < PAIRS:
                        evac(9 + EARLY + p)
                    pt_copy(Q + p)
                    if p + 2 < PAIRS:
                        exps(Q + p + 2)
                    out_hi(Q + p, p)
                mixer_out(layer)

            def act_rwkv(layer):
                s0 = first_slab[layer, "mix"]
                act.wait_ge(shift_turned, 1)
                act.copy(shot[:, :], psum[6][0:16, 0:128]).then_inc(shift_out, 1)
                done = done_after[s0 - 1]
                for i in range(24):
                    if i % 2 == 0 and i < 22:
                        split_hi(s0 + i // 2 + 1)
                    act.wait_ge(mm_done, done + i + 1)
                    act.copy((R, K, VV)[i // 8][:, i % 8, :], psum[i % 4][:, 0:T]).then_inc(rkv_evac, 1)
                for a in range(3):
                    r_ = (slice(0, 64), slice(64, 128), slice(0, 128))[a]
                    act.wait_ge(lora_mid, a + 1)
                    act.activation((LTg if a == 2 else LT)[r_, :], psum[4 + a][r_, 0:T], (ACT.Tanh, ACT.Copy, ACT.Sigmoid)[a]
                                   ).then_inc(lora_act, 1)
                    for m in range(KD):
                        act.wait_ge(lora_out, 8 * a + m + 1)
                        ps = psum[(8 * a + m) % 4][:, 0:T]
                        if a < 2:
                            act.activation((LW, A)[a][:, m, :], ps, ACT.Sigmoid, bias=vcol(("b_w0", "b_a0")[a], m)).then_inc(lora_evac, 1)
                        else:
                            act.copy(G[:, m, :], ps).then_inc(lora_evac, 1)
                act.wait_ge(cc_done, 1)
                act.activation(T1[:, :, :], HN[:, :, :], ACT.Exp)
                act.activation(T2[:, :, :], HN[:, :, :], ACT.Exp, scale=-1.0).then_inc(decay_done, 1)
                act.wait_ge(lwp_done, 1)
                act.activation(LW[:, :, :], LW[:, :, :], ACT.Exp).then_inc(prev_done, 1)
                act.wait_ge(kk_raw, 1)
                act.activation(XX[:, :, :], MX[:, :, :], ACT.Square).then_inc(kk_sq, 1)
                for k in range(KD):
                    act.wait_ge(hs_done, k + 1)
                    act.activation(XX[:, k, :], psum[k % 4][:, 0:T], ACT.Sqrt).then_inc(hs_root, 1)
                for g in range(2):
                    act.wait_ge(state_turned, g + 1)
                    act.copy(BX[g][3][:, :, :], psum[4 * g][:, :].rearrange("p (q n) -> p q n", q=4)).then_inc(state_set, 1)
                for c in range(CHUNKS):
                    for z, (name, e_, _) in enumerate(STAGES):
                        if "a" not in e_:
                            continue
                        for g in range(2):
                            act.wait_ge(stage_pe[g], len(STAGES) * c + z + 1)
                            bank = psum[4 * g + z % 4]
                            dst = {"vt": BX[g][0], "bt": BX[g][1], "kt": BX[g][2], "m2": BD[g][1], "m2T": BD[g][2], "m4": BD[g][5],
                                   "m4T": BD[g][4], "m8": BD[g][1], "qT": BD[g][4], "q": BD[g][5], "q2": BD[g][1],
                                   "rhs": BD[g][4], "x1": BD[g][5], "u": BD[g][1]}.get(name)
                            if name == "y":
                                act.copy(R[:, 4 * g:4 * g + 4, 64 * c:64 * c + 64],
                                         bank[:, 0:256].rearrange("p (q n) -> p q n", q=4)).then_inc(stage_act[g], 1)
                            else:
                                act.copy(dst[:, :, :], bank[:, :].rearrange("p (q n) -> p q n", q=4)).then_inc(stage_act[g], 1)
                    if c in (0, CHUNKS - 1):
                        for g in range(2):
                            act.wait_ge(z_turned, 2 * (c > 0) + g + 1)
                            act.copy((BD[0][4 + g] if c else SS[g])[:, :, :], psum[4 * g][:, :].rearrange("p (q n) -> p q n", q=4)
                                     ).then_inc(z_staged, 1)
                split_hi(first_slab[layer, "out"])
                act.wait_ge(state_stored, 64)
                for k in range(KD):
                    act.wait_ge(y_mean, k + 1)
                    act.activation(MX[:, k, :], R[:, k, :], ACT.Square).then_inc(y_sq, 1)
                for k in range(KD):
                    act.wait_ge(hs_done, 24 + k + 1)
                    act.activation(MX[:, k, :], psum[k % 4][:, 0:T], ACT.Sqrt, bias=C("eps")[:, 1:2], scale=1.0 / 64).then_inc(y_root, 1)
                mixer_out(layer)

            def act_mla(layer):
                s0 = first_slab[layer, "mix"]
                E, Rb, Q = E0[layer], R0[layer], Q0[layer]
                done = done_after[s0 - 1]
                nq, nkv = norm_of[layer, "cq"], norm_of[layer, "ckv"]

                def evac(e_, dst, rows, cols_, b):
                    act.wait_ge(mm_done, done + e_ + 1)
                    act.copy(dst, psum[b][0:rows, 0:cols_]).then_inc(tile_evac, 1)

                for t in range(7):
                    if t in (0, 2, 4):
                        split_hi(s0 + t // 2 + 1)
                    if t == 0:
                        root(norm_of[layer, "mix"])
                    if t < 6:
                        square(nq if t < 4 else nkv, t if t < 4 else t - 4, CQ[:, t, :], lambda: act.wait_ge(tile_evac, E + t + 1))
                act.wait_ge(perm_done, Rb + 1)
                act.copy(qraw[0:96, Rb % 2, :], psum[3][0:96, 0:T]).then_inc(placed, 1)
                root(nq)
                act.wait_ge(cqn_done, 1)
                root(nkv)
                for z, (c, n_) in enumerate(TILES):
                    act.wait_ge(rows_turned, ROWS_BEFORE[layer] + z + 1)
                    b = psum[(7, 6, 4)[z]]
                    act.copy(lato[0:n_, z, :], b[0:n_, 0:256])
                    act.copy(ropeo[0:n_, z, :], b[0:n_, 256:352]).then_inc(rows_out, 1)
                for j in range(2):
                    split_hi(s0 + 4 + j)
                    for st in range(4):
                        e_ = 7 + 12 * j + st
                        evac(e_, VC[:, st, 512 * j:512 * j + 512], 128, 512, 0 if e_ % 2 == 0 else 2)
                    for h in range(8):
                        e_ = 11 + 12 * j + h
                        evac(e_, KC[0:64, 8 * j + h, :], 64, KEYS, 0 if e_ % 2 == 0 else 2)

                def head(h):
                    r = Rb + 1 + h
                    act.wait_ge(perm_done, r - 1)
                    act.wait_ge(cos_done, r - 1)
                    evac(31 + h, qraw[0:96, r % 2, :], 96, T, 0)
                    if h % 4 == 0:
                        split_hi(s0 + 6 + h // 4)

                for h in range(4):
                    head(h)
                exps(Q)
                for p in range(PAIRS):
                    if p + 2 < PAIRS:
                        head(2 * p + 4)
                    pt_copy(Q + p)
                    if p + 1 < PAIRS:
                        exps(Q + p + 1)
                    if p + 2 < PAIRS:
                        head(2 * p + 5)
                    out_hi(Q + p, p)
                mixer_out(layer)

            for layer in range(DEPTH):
                (dsa, act_rwkv, act_mla)[layer % 3](layer)
                ffn(layer)

            for k in range(KD):
                act.wait_ge(y_turned, k + 1)
                c_ = slice(128 * k, 128 * k + 128)
                act.copy(xin[0:64, 0, c_], psum[k % 2][0:64, 0:128])
                act.copy(xin[:, 1:3, c_], psum[k % 2][:, 128:384].rearrange("p (z q) -> p z q", z=2)).then_inc(y_copied, 1)

        @block.vector
        def _(dve):
            chain = Chain(dve, dve_c)

            def split_lo(n, count=None):
                s_ = slabs[n]
                dve.wait_ge(w_hi, n + 1 if count is None else count)
                w_ = s_.kt * s_.w
                dve.tensor_tensor(lo[n % 2][:, 0:w_], raw[n % 2][:, 0:w_], hi[n % 2][:, 0:w_].bitcast(F32),
                                  ALU.subtract).then_inc(w_lo, 1)

            def scale_of(j):
                dve.wait_ge(rms_done, j + 1)
                dve.reciprocal(rstd[:, :], rms[:, :]).then_inc(rstd_done, 1)
                dve.wait_ge(rstd_done, j + 1)

            def x_parts(j, k, c=None):
                c = k if c is None else c
                x, xh, xl = (t_[:, bass.ds(c, 1), :].rearrange("p o n -> p (o n)") for t_ in (xT, XH, XL))
                name, l_ = GAIN[j]
                g_ = V[:, bass.ds(c + (VOFF[name] + 8 * l_), 1)]
                dve.wait_ge(x_done, c + (8 * xs_of[j] + 1))
                dve.tensor_scalar(xh, x, g_, None, ALU.mult).then_inc(xh_done, 1)
                dve.wait_ge(xh_done, c + (XN[j] + 1))
                dve.scalar_tensor_tensor(out=xl, in0=x, scalar=g_, in1=xh.bitcast(F32), op0=ALU.mult, op1=ALU.subtract).then_inc(xn_done, 1)

            for k in range(KD):
                dve.wait_ge(xt_ready, k + 1)
                dve.tensor_copy(xT[:, k, :], psum[k % 2][:, 0:T]).then_inc(x_done, 1)
            split_lo(0)
            dve.wait_ge(v_copied, VGROUPS)
            dve.wait_ge(con_in, 16)
            for k in range(KD):
                x_parts(0, k)

            def rope(q, dst, rows=128):
                dve.wait_ge(perm_done, q + 1)
                chain(dve.tensor_tensor(qsin[0:rows, :], psum[1][0:rows, 0:T], sinr[:, :] if rows == 128 else C("sin_c", rows), ALU.mult))
                dve.wait_ge(cos_done, q + 1)
                dve.tensor_tensor(dst, qcos[0:rows, q % 2, :], qsin[0:rows, :], ALU.add).then_inc(rope_done, 1)

            def maxima(q, masks, scale):
                dve.wait_ge(qk_done, q + 1)
                back = 2 if PAIRS <= q < 2 * PAIRS else 3
                if q >= back:
                    dve.wait_ge(pt_turned, q - back + 1)
                src = [psum[3][:, 0:128], psum[3][:, 128:384], psum[4][:, 0:128], psum[4][:, 128:384], psum[5][:, 0:192]]
                for u, (a, b) in enumerate(UNITS):
                    ins = dve.tensor_tensor_reduce(LS(q)[:, a:b], src[u], masks[u], -scale, 3.0e38, ALU.add, ALU.min,
                                                   negmax[:, slot(q), u:u + 1])
                ins.then_inc(max_done, 1)

            def probs(q):
                dve.wait_ge(exp_done, q + 1)
                chain(dve.reciprocal(rsum[:, slot(q), 0:5], sums[:, slot(q), 0:5]))
                for u, (a, b) in enumerate(UNITS):
                    ins = dve.tensor_scalar(LS(q)[:, a:b], LS(q)[:, a:b], rsum[:, slot(q), u:u + 1], None, ALU.mult)
                ins.then_inc(prob_done, 1)

            def pt_copy(q):
                dve.wait_ge(pt_turned, q + 1)
                if q:
                    dve.wait_ge(pv_done, q)
                dve.tensor_copy(PT[:, 0:512], psum[6][:, 0:512]).then_inc(pt_dve, 1)

            def out_lo(q, p):
                dve.wait_ge(oh_done, q + 1)
                dve.tensor_tensor(OL[:, p, :], psum[2][:, 0:T], OH[:, p, :].bitcast(F32), ALU.subtract).then_inc(ol_done, 1)

            def mixer_out(layer):
                s0 = first_slab[layer, "out"]
                for m in range(KD):
                    if m % 2 == 0:
                        split_lo(s0 + m // 2 + 1)
                    dve.wait_ge(mm_done, done_after[s0 - 1] + m + 1)
                    dve.tensor_tensor(xT[:, m, :], xT[:, m, :], psum[4 + m % 2][:, 0:T], ALU.add).then_inc(x_done, 1)
                    if layer % 3 != 1:
                        x_parts(norm_of[layer, "ffn"], m)
                for m in range(KD if layer % 3 == 1 else 0):
                    x_parts(norm_of[layer, "ffn"], m)

            def ffn(layer):
                F0 = NF * layer
                u0, d0 = first_slab[layer, "up"], first_slab[layer, "down"]
                def gate(f, j):
                    dve.wait_ge(silu_done, f + F0)
                    dve.tensor_tensor(gated[:, :], silu[:, :], conv[:, 1 - j, 1, :], ALU.mult).then_inc(ffn_step, 1)
                    dve.wait_ge(ffn_step, (f + (F0 - 1)) * 6 + 5)
                    gh = GH[:, bass.ds(f + -1, 1), :].rearrange("p o n -> p (o n)")
                    gl = GL[:, bass.ds(f + -1, 1), :].rearrange("p o n -> p (o n)")
                    dve.tensor_copy(gh, gated[:, :]).then_inc(ffn_step, 1)
                    dve.wait_ge(ffn_step, (f + (F0 - 1)) * 6 + 6)
                    dve.tensor_tensor(gl, gated[:, :], gh.bitcast(F32), ALU.subtract).then_inc(g_done, 1)

                split_lo(u0 + 1)
                scale_of(norm_of[layer, "ffn"])

                def step(f, j, n_later, hi_count, first):
                    split_lo(n_later, hi_count)
                    if not first:
                        gate(f, j)
                    dve.wait_ge(c2_done, f + (F0 + 1))
                    dve.wait_ge(hist_done, f + (F0 + 1))
                    for tap in (1, 0):
                        w_ = VOFF["f_w_conv"] + (layer * 3 + tap) * 44
                        for h in range(2):
                            if tap == 0:
                                dve.wait_ge(ffn_step, (f + F0) * 6 + 1 + h)
                            dve.scalar_tensor_tensor(out=conv[:, j, h, :], in0=upad[:, j, h, tap:tap + TG],
                                                     scalar=V[:, bass.ds(f + (w_ + NF * h), 1)], in1=conv[:, j, h, :],
                                                     op0=ALU.mult, op1=ALU.add).then_inc(ffn_step, 1)

                for j in range(2):
                    step(j, j, u0 + j + 2, None, j == 0)
                with dve.Fori(1, NF // 2 - 1) as i:
                    for j in range(2):
                        step(i * 2 + j, j, u0 + 2 + j + 2, i * 2 + (u0 + j + 3), False)
                for j in range(2):
                    step(NF - 2 + j, j, u0 + NF - 2 + j + 2, None, False)
                gate(NF, 0)
                jn = norm_next(layer)

                def down(m, k, hi_count, mm_count):
                    for half in range(2):
                        n = d0 + 2 * k + half + 1
                        if n > d0 + 1 and n < N:
                            split_lo(n, hi_count and hi_count(half))
                    dve.wait_ge(mm_done, mm_count)
                    x = xT[:, bass.ds(m, 1), :].rearrange("p o n -> p (o n)")
                    ps = psum[4 + k % 2]
                    dve.tensor_tensor(x[:, 0:64], x[:, 0:64], ps[:, 0:64], ALU.add)
                    dve.tensor_tensor(x[:, 64:T], x[:, 64:T], ps[:, 66:TG], ALU.add).then_inc(x_done, 1)
                    if jn in LATE:
                        x_parts(jn, None, m)

                for m in range(2):
                    down(m, m, None, done_after[d0 + 2 * m + 1])
                with dve.Fori(1, KD // 2 - 1) as i:
                    for j in range(2):
                        down(i * 2 + j, 2 + j, lambda half: i * 4 + (d0 + 2 * j + half + 2),
                             i * 4 + (done_after[d0 + 2 * j + 1]))
                for m in (KD - 2, KD - 1):
                    down(m, m, None, done_after[d0 + 2 * m + 1])

            def dsa(layer):
                inst, s0 = layer // 3, first_slab[layer, "mix"]
                E, Rb, Q = E0[layer], R0[layer], Q0[layer]
                new = slice(PAST, KEYS)
                dsts = [KT[:, 0, new], KT[:, 1, new], KIT[:, new], QIT[:, 0, :], QIT[:, 1, :], QIT[:, 2, :], QIT[:, 3, :]]
                lo_at = {0: 1, 2: 2, 3: 3, 5: 4}
                for r in range(7):
                    if r in lo_at:
                        split_lo(s0 + lo_at[r])
                    if r == 0:
                        scale_of(norm_of[layer, "mix"])
                        chain(dve.tensor_tensor(sinr[:, :], C("sin_a"), rstd[:, :], ALU.mult))
                    if r == 4:
                        dve.wait_ge(tile_evac, E + 5)
                        dve.tensor_tensor(WIf[:, :], WIf[:, :], rstd[:, :], ALU.mult)
                        dve.tensor_tensor(VTf[:, :], VTf[:, :], rstd[:, :], ALU.mult).then_inc(rows_scaled, 1)
                    rope(Rb + r, dsts[r])
                dve.wait_ge(turned, inst + 1)
                dve.tensor_copy(KT[:, :, 0:PAST], psum[3][:, 0:256].rearrange("p (g n) -> p g n", g=2))
                dve.tensor_copy(KIT[:, 0:PAST], psum[3][:, 256:384]).then_inc(turned_in, 1)
                parts = ((0, 128, 0, 128), (1, 128, 128, 384), (2, 64, 384, 576))
                wi_of = (1, 2, 0)
                for h in range(8):
                    dve.wait_ge(relu_done, 8 * inst + h + 1)
                    if h:
                        dve.wait_ge(score_done, 8 * inst + h)
                    for z, n_, a, b in parts:
                        w_ = WI[0:n_, wi_of[z], h:h + 1]
                        if h == 0:
                            ins = dve.tensor_scalar(SC[0:n_, a:b], relu[0:n_, 0, a:b], w_, None, ALU.mult)
                        else:
                            ins = dve.scalar_tensor_tensor(out=SC[0:n_, a:b], in0=relu[0:n_, h % 2, a:b], scalar=w_,
                                                           in1=SC[0:n_, a:b], op0=ALU.mult, op1=ALU.add)
                    ins.then_inc(score_done, 1)
                dve.wait_ge(score_done, 8 * inst + 8)
                dve.scalar_tensor_tensor(out=SW[:, 0:128], in0=SC[:, 0:128], scalar=I_SCALE, in1=C("valid0"), op0=ALU.mult, op1=ALU.add)
                dve.scalar_tensor_tensor(out=SW[:, 128:384], in0=SC[:, 128:384], scalar=I_SCALE, in1=C("valid1"), op0=ALU.mult, op1=ALU.add)
                chain(dve.tensor_scalar(SW[0:64, 384:576], SC[0:64, 384:576], I_SCALE, None, ALU.mult))
                for r in range(8):
                    live = parts if r < 6 else parts[:2]
                    for z, n_, a, b in live:
                        ins = dve.max(top8[0:n_, z, :], SW[0:n_, a:b])
                    chain(ins)
                    for z, n_, a, b in live:
                        ins = dve.match_replace(SW[0:n_, a:b], top8[0:n_, z, :], SW[0:n_, a:b], REPLACED)
                    chain(ins)
                    if r % 2 == 0 and r < EARLY:
                        split_lo(s0 + 5 + r // 2)
                    if r < EARLY:
                        rope(Rb + 7 + r, QD[:, r, :])
                dve.tensor_scalar(MK[:, 0:384], SW[:, 0:384], -3.0e38, OFF, ALU.is_gt, ALU.mult)
                dve.tensor_scalar(MK[0:64, 384:576], SW[0:64, 384:576], -3.0e38, OFF, ALU.is_gt, ALU.mult).then_inc(mask_done, 1)
                dve.wait_ge(mask_done, inst + 1)
                dve.wait_ge(mask_copied, 16 * (inst + 1))
                masks = [MK[:, 0:128], MK[:, 128:384], MK[:, 0:128], MK[:, 128:384], MK[:, 384:576]]
                maxima(Q, masks, A_SCALE)
                maxima(Q + 1, masks, A_SCALE)
                probs(Q)
                for p in range(PAIRS):
                    pt_copy(Q + p)
                    if p + 2 < PAIRS:
                        maxima(Q + p + 2, masks, A_SCALE)
                    if p + EARLY < PAIRS:
                        rope(Rb + 7 + EARLY + p, QD[:, EARLY + p, :])
                    if (p + EARLY) % 2 == 0 and p + EARLY < PAIRS:
                        split_lo(s0 + 5 + (p + EARLY) // 2)
                    if p + 1 < PAIRS:
                        probs(Q + p + 1)
                    out_lo(Q + p, p)
                mixer_out(layer)

            def over_pairs(name, n_=4):
                m_ = C(name)
                return m_.rearrange("p (o n) -> p o n", o=1).to_broadcast([128, n_, m_.shape[1]])

            def dve_rwkv(layer):
                s0 = first_slab[layer, "mix"]
                j = norm_of[layer, "mix"]
                scale_of(j)
                for k in range(KD):
                    ins = dve.scalar_tensor_tensor(out=HN[:, k, :], in0=xT[:, k, :], scalar=gain(GAIN[j], k), in1=rstd[:, :],
                                                   op0=ALU.mult, op1=ALU.mult)
                chain(ins)
                dve.tensor_copy(sho[:, 0:8], HN[:, :, 63])
                dve.tensor_copy(sho[:, 8:16], HN[:, :, T - 1]).then_inc(shift_set, 1)
                chain(dve.tensor_tensor(XX[:, :, 1:T], HN[:, :, 0:T - 1], HN[:, :, 1:T], ALU.subtract))
                dve.tensor_tensor(XX[:, :, 0], V[:, VOFF["state_b_shift"]:VOFF["state_b_shift"] + 8], HN[:, :, 0], ALU.subtract)
                chain(dve.tensor_scalar(XX[:, :, 64], HN[:, :, 64], -1.0, None, ALU.mult))

                def mix(mu):
                    for k in range(KD):
                        ins = dve.scalar_tensor_tensor(out=MX[:, k, :], in0=XX[:, k, :], scalar=vcol("b_mu", 8 * mu + k),
                                                       in1=HN[:, k, :], op0=ALU.mult, op1=ALU.add)
                    return ins

                for m, mu in enumerate((0, 2, 3)):
                    chain(mix(mu))
                    if m:
                        dve.wait_ge(mm_done, done_after[s0 + 4 * m - 1])
                    chain(dve.tensor_copy(XH[:, :, :], MX[:, :, :]))
                    dve.tensor_tensor(XL[:, :, :], MX[:, :, :], XH[:, :, :].bitcast(F32), ALU.subtract).then_inc(mix_done, 1)
                    for n in range(4 * m + 1, 4 * m + 5):
                        if n < 12:
                            split_lo(s0 + n)
                for a, mu in enumerate((1, 4, 5)):
                    if a:
                        dve.wait_ge(lora_mid, a)
                    mix(mu).then_inc(mix_done, 1)
                dve.wait_ge(lora_mid, 3)
                dve.wait_ge(rkv_evac, 24)
                for k in range(KD):
                    ins = dve.tensor_scalar(MX[:, k, :], K[:, k, :], vcol("b_k_k", k), None, ALU.mult)
                ins.then_inc(kk_raw, 1)
                dve.wait_ge(lw_done, 1)
                for k in range(KD):
                    ins = dve.tensor_tensor_scan(HN[:, k, :], C("scan_keep"), LW[:, k, :], 0.0, ALU.mult, ALU.add)
                ins.then_inc(cc_done, 1)
                dve.wait_ge(cc_done, 1)
                dve.tensor_tensor(LW[:, :, :], HN[:, :, :], LW[:, :, :], ALU.subtract).then_inc(lwp_done, 1)
                dve.wait_ge(lora_evac, 16)
                ka = V[:, VOFF["b_k_a"]:VOFF["b_k_a"] + 8]
                chain(dve.tensor_scalar(onemka[:, :], ka, -1.0, 1.0, ALU.mult, ALU.add))
                for k in range(KD):
                    t = xn[:, k % 2, :]
                    chain(dve.tensor_scalar(t, A[:, k, :], vcol("b_k_a", k), onemka[:, k:k + 1], ALU.mult, ALU.add))
                    ins = dve.tensor_tensor(K[:, k, :], K[:, k, :], t, ALU.mult)
                chain(ins)
                dve.wait_ge(hs_root, 8)
                chain(dve.tensor_scalar(XX[:, :, :], XX[:, :, :], 1e-12, None, ALU.max))
                chain(dve.reciprocal(XX[:, :, :], XX[:, :, :]))
                chain(dve.tensor_tensor(MX[:, :, :], MX[:, :, :], XX[:, :, :], ALU.mult))
                for k in range(KD):
                    dve.scalar_tensor_tensor(out=XX[:, k, :], in0=R[:, k, :], scalar=vcol("b_r_k", k), in1=K[:, k, :],
                                             op0=ALU.mult, op1=ALU.mult).then_inc(bonus_in, 1)
                chain(dve.tensor_tensor(A[:, :, :], MX[:, :, :], A[:, :, :], ALU.mult))
                for k in range(KD):
                    dve.wait_ge(hs_done, 8 + k + 1)
                    dve.tensor_tensor(XX[:, k, :], psum[k % 4][:, 0:T], VV[:, k, :], ALU.mult).then_inc(bonus_out, 1)
                dve.wait_ge(decay_done, 1)
                dve.tensor_copy(Dend[:, :, :], T1[:, :, 63:T:64])
                dve.tensor_tensor(A[:, :, :], A[:, :, :], T2[:, :, :], ALU.mult)
                dve.tensor_tensor(K[:, :, :], K[:, :, :], T2[:, :, :], ALU.mult)
                dve.tensor_tensor(R[:, :, :], R[:, :, :], T1[:, :, :], ALU.mult)
                dve.wait_ge(prev_done, 1)
                f_ = [t[:, :, :].rearrange("p k n -> p (k n)") for t in (MX, LW)]
                dve.scalar_tensor_tensor(out=f_[0], in0=f_[0], scalar=-1.0, in1=f_[1], op0=ALU.mult, op1=ALU.mult).then_inc(rec_ready, 1)
                dve.wait_ge(rec_ready, 1)
                dve.wait_ge(built_pool, 1)
                for c in range(CHUNKS):
                    for g in range(2):
                        if c:
                            taken(dve, g, c - 1, 22)
                            taken(dve, g, c - 1, 23)
                        for z, src in ((1, A), (2, K)):
                            for e in range(2):
                                r_ = slice(64 * e, 64 * e + 64)
                                ins = dve.tensor_copy(BD[g][z][r_, :, r_], src[r_, 4 * g:4 * g + 4, 64 * c:64 * c + 64])
                        ins.then_inc(built_dve, 1)
                    for z, (name, e_, _) in enumerate(STAGES):
                        if "d" not in e_:
                            continue
                        for g in range(2):
                            dve.wait_ge(stage_pe[g], len(STAGES) * c + z + 1)
                            b = BD[g]
                            bank = psum[4 * g + z % 4][:, :].rearrange("p (q n) -> p q n", q=4)
                            if name == "mT":
                                chain(dve.tensor_tensor(b[4][:, :, :], bank, over_pairs("mt_diag"), ALU.mult))
                                ins = dve.tensor_tensor(b[9][:, :, :], b[4][:, :, :], over_pairs("ident"), ALU.add)
                            elif name == "m":
                                dve.tensor_tensor(b[5][:, :, :], bank, over_pairs("m_diag"), ALU.mult)
                                ins = dve.tensor_tensor(b[6][:, :, :], bank, over_pairs("m_off"), ALU.mult)
                            elif name == "nT":
                                ins = dve.tensor_tensor(b[7][:, :, :], bank, over_pairs("mt_strict"), ALU.mult)
                            elif name == "arT":
                                ins = dve.tensor_tensor(b[8][:, :, :].rearrange("p a (b n) -> p (a b) n", n=64),
                                                        psum[4 * g + z % 4][:, :].rearrange("p (q n) -> p q n", q=8),
                                                        over_pairs("mt_incl", 8), ALU.mult)
                            elif name in ("p2", "p4", "p8", "h"):
                                old, new = {"p2": (9, 3), "p4": (3, 9), "p8": (9, 3), "h": (2, 9)}[name]
                                ins = dve.tensor_tensor(b[new][:, :, :], bank, b[old][:, :, :], ALU.add)
                            elif name == "qT":
                                dve.wait_ge(stage_act[g], c * ACT_STAGES + ACT_AT[z])
                                ins = dve.tensor_tensor(b[2][:, :, :], b[4][:, :, :], over_pairs("ident"), ALU.add)
                            else:
                                Z = BX[g][3]
                                chain(dve.tensor_tensor(Z[:, :, :], bank, Z[:, :, :], ALU.add))
                                for q in range(4):
                                    ins = dve.tensor_scalar(Z[:, q, :], Z[:, q, :], Dend[:, 4 * g + q, c:c + 1], None, ALU.mult)
                            ins.then_inc(stage_dve[g], 1)
                    if c == 0:
                        for g in range(2):
                            dve.wait_ge(z_turned, g + 1)
                            dve.memset(BX[g][3][:, :, :], 0.0).then_inc(state_set, 1)
                dve.wait_ge(z_turned, 4)
                dve.sem_inc(rec_done, 1)
                split_lo(first_slab[layer, "out"])
                for k in range(KD):
                    dve.wait_ge(hs_done, 16 + k + 1)
                    dve.scalar_tensor_tensor(out=R[:, k, :], in0=psum[k % 4][:, 0:T], scalar=-1.0 / 64, in1=R[:, k, :],
                                             op0=ALU.mult, op1=ALU.add).then_inc(y_mean, 1)
                dve.wait_ge(y_mean, 8)
                dve.wait_ge(z_staged, 4)
                for k in range(KD + 1):
                    if k < KD:
                        dve.wait_ge(y_root, k + 1)
                        dve.reciprocal(MX[:, k, :], MX[:, k, :]).then_inc(y_inv, 1)
                    if k:
                        dve.wait_ge(y_gated, k)
                        chain(dve.tensor_copy(XH[:, k - 1, :], R[:, k - 1, :]))
                        dve.tensor_tensor(XL[:, k - 1, :], R[:, k - 1, :], XH[:, k - 1, :].bitcast(F32), ALU.subtract).then_inc(y_parts, 1)
                mixer_out(layer)

            def dve_mla(layer):
                s0 = first_slab[layer, "mix"]
                E, Rb, Q = E0[layer], R0[layer], Q0[layer]
                split_lo(s0 + 1)
                scale_of(norm_of[layer, "mix"])
                for t in range(7):
                    dve.wait_ge(mm_done, done_after[s0 - 1] + t + 1)
                    dst = CQ[:, t, :] if t < 6 else qraw[:, Rb % 2, :]
                    dve.tensor_tensor(dst, psum[0 if t % 2 == 0 else 2][:, 0:T], rstd[:, :], ALU.mult).then_inc(tile_evac, 1)
                    if t in (1, 3):
                        split_lo(s0 + 2 + t // 2)
                rope(Rb, KPE[:, :], 96)
                dve.wait_ge(mla_turned, 1)
                dve.tensor_copy(LATF[:, :, 0:PAST], psum[6][:, 0:256].rearrange("p (k n) -> p k n", k=2))
                crt = psum[6][64:96, 256:384].rearrange("p (o n) -> p o n", o=1).to_broadcast([32, 16, PAST])
                dve.tensor_copy(KC[64:96, :, 0:PAST], crt).then_inc(mla_cached, 1)
                scale_of(norm_of[layer, "cq"])
                dve.wait_ge(mm_done, done_after[s0 + 2])
                for k in range(4):
                    t = xn[:, k % 2, :]
                    chain(dve.scalar_tensor_tensor(out=t, in0=CQ[:, k, :], scalar=vcol("c_g_q", k), in1=rstd[:, :],
                                                   op0=ALU.mult, op1=ALU.mult))
                    chain(dve.tensor_copy(XH[:, k, :], t))
                    dve.tensor_tensor(XL[:, k, :], t, XH[:, k, :].bitcast(F32), ALU.subtract).then_inc(cqn_done, 1)
                scale_of(norm_of[layer, "ckv"])
                for k in range(2):
                    dve.scalar_tensor_tensor(out=LATF[:, k, PAST:KEYS], in0=CQ[:, 4 + k, :], scalar=vcol("c_g_kv", k), in1=rstd[:, :],
                                             op0=ALU.mult, op1=ALU.mult).then_inc(latf_done, 1)
                dve.wait_ge(latf_done, 2)
                dve.wait_ge(mla_cached, 1)
                chain(dve.tensor_copy(LATH, LATF[:, :, :]))
                dve.tensor_tensor(LATL, LATF[:, :, :], LATH.bitcast(F32), ALU.subtract).then_inc(lat_parts, 1)
                split_lo(s0 + 4)
                split_lo(s0 + 5)

                def head(h):
                    rope(Rb + 1 + h, QT[0:96, (h // 2) % 2, h % 2, :], 96)
                    if h % 4 == 0:
                        split_lo(s0 + 6 + h // 4)

                for h in range(4):
                    head(h)
                masks = [C("off0"), C("off1"), C("off0"), C("off1"), C("zero")]
                maxima(Q, masks, C_SCALE)
                probs(Q)
                for p in range(PAIRS):
                    pt_copy(Q + p)
                    if p + 1 < PAIRS:
                        maxima(Q + p + 1, masks, C_SCALE)
                    if p + 2 < PAIRS:
                        head(2 * p + 4)
                    if p + 1 < PAIRS:
                        probs(Q + p + 1)
                    out_lo(Q + p, p)
                    if p + 2 < PAIRS:
                        head(2 * p + 5)
                mixer_out(layer)

            for layer in range(DEPTH):
                (dsa, dve_rwkv, dve_mla)[layer % 3](layer)
                ffn(layer)

            scale_of(norm_final)
            for k in range(KD):
                if k >= 2:
                    dve.wait_ge(y_turned, k - 1)
                dve.scalar_tensor_tensor(out=xn[:, k % 2, :], in0=xT[:, k, :], scalar=gain(GAIN[norm_final], k), in1=rstd[:, :],
                                         op0=ALU.mult, op1=ALU.mult).then_inc(xn_done, 1)


_NAMES = ["x_prompt", "x_sample", "cache_a_k", "cache_a_v", "cache_a_idx", "state_b_wkv", "state_b_shift", "cache_c_latent",
          "cache_c_rope", "state_ffn_conv", "n_mix", "n_ffn", "n_final", "a_w_in", "a_w_out", "b_mu", "b_w_rkv", "b_w0",
          "b_w1", "b_w2", "b_a0", "b_a1", "b_a2", "b_g1", "b_g2", "b_k_k", "b_k_a", "b_r_k", "b_ln_w", "b_ln_b", "b_w_out",
          "c_w_in", "c_g_q", "c_g_kv", "c_w_uq", "c_w_ukv", "c_w_out", "f_w_up", "f_w_conv", "f_b_conv", "f_w_down"]
_OUTS = [("y_prompt", (1, 256, 1024)), ("y_sample", (1, 64, 1024)), ("a_k_prompt", (2, 1, 256, 2, 64)),
         ("a_k_sample", (2, 1, 64, 2, 64)), ("a_v_prompt", (2, 1, 256, 2, 64)), ("a_v_sample", (2, 1, 64, 2, 64)),
         ("a_idx_prompt", (2, 1, 256, 64)), ("a_idx_sample", (2, 1, 64, 64)), ("b_wkv_prompt", (1, 1, 16, 64, 64)),
         ("b_wkv_sample", (1, 1, 16, 64, 64)), ("b_shift_prompt", (1, 1, 1024)), ("b_shift_sample", (1, 1, 1024)),
         ("c_lat_prompt", (1, 1, 256, 256)), ("c_lat_sample", (1, 1, 64, 256)), ("c_rope_prompt", (1, 1, 256, 32)),
         ("c_rope_sample", (1, 1, 64, 32)), ("ffn_prompt", (4, 1, 2, 5632)), ("ffn_sample", (4, 1, 2, 5632))]


def kernel(**inputs):
    import concourse.bacc as bacc
    from concourse.bass_utils import run_bass_kernel_spmd

    nc = bacc.Bacc("TRN2", target_bir_lowering=False, num_devices=1)
    arrays, ins, outs = {}, {}, {}
    for name in _NAMES:
        a = np.ascontiguousarray(inputs[name])
        arrays[f"in_{name}"] = a
        ins[name] = nc.dram_tensor(f"in_{name}", a.shape, F32, kind="ExternalInput").ap()
    arrays["in_const"] = constants()
    ins["const"] = nc.dram_tensor("in_const", arrays["in_const"].shape, F32, kind="ExternalInput").ap()
    for name, shape in _OUTS:
        outs[name] = nc.dram_tensor(f"out_{name}", shape, F32, kind="ExternalOutput").ap()
    build(nc, ins, outs)
    r = run_bass_kernel_spmd(nc, [arrays], core_ids=[0])
    return tuple(r.results[0][f"out_{name}"] for name, _ in _OUTS)
```
